# Optimizing a Trainium2 kernel written in Bass

```python
import math
import jax, jax.numpy as jnp
from jax import lax
import numpy as np

D_MODEL = 1024
BATCH = 1
SEQ = 256
DEPTH = 2

D_FF = 2816
ALPHA = (2 * DEPTH) ** 0.25
BETA = (8 * DEPTH) ** -0.25
LN_EPS = 1e-5
NEG = -1e30

A_HEADS = 8
A_DH = 64
A_WIDTH = A_HEADS * A_DH
MOBA_BLOCK = 256
MOBA_TOPK = 3
MOBA_QCHUNK = 64
ROPE_THETA = 10000.0

B_GROUPS = 8
B_DG = 64
B_WIDTH = B_GROUPS * B_DG
SGU_CHUNK = 128
AB_IN = 3 * A_WIDTH + 2 * B_WIDTH
AB_MIX = A_WIDTH + B_WIDTH

C_HEADS = 4
C_DQK = 128
C_DV = 256
C_QK_WIDTH = C_HEADS * C_DQK
C_WIDTH = C_HEADS * C_DV
C_IN = 2 * C_QK_WIDTH + 2 * C_WIDTH + 2 * C_HEADS
MLSTM_CHUNK = 64
CONV_W = 4


def layer_norm(x, g, b):
    xf = x.astype(jnp.float32)
    mu = jnp.mean(xf, axis=-1, keepdims=True)
    var = jnp.mean(jnp.square(xf - mu), axis=-1, keepdims=True)
    y = (xf - mu) * lax.rsqrt(var + LN_EPS) * g.astype(jnp.float32) + b.astype(jnp.float32)
    return y.astype(x.dtype)

def swiglu(x, w_gu, w_down):
    g, u = jnp.split(x @ w_gu, 2, axis=-1)
    return (jax.nn.silu(g) * u) @ w_down

def rotary(x, pos):
    half = x.shape[-1] // 2
    inv = ROPE_THETA ** (-jnp.arange(half, dtype=jnp.float32) / half)
    ang = pos.astype(jnp.float32)[:, None] * inv[None, :]
    cos, sin = jnp.cos(ang), jnp.sin(ang)
    xf = x.astype(jnp.float32)
    x1, x2 = xf[..., :half], xf[..., half:]
    return jnp.concatenate([x1 * cos - x2 * sin, x2 * cos + x1 * sin], axis=-1).astype(x.dtype)

def moba_attention(q, k, v):
    Bn, H, S, dh = q.shape
    nb = -(-S // MOBA_BLOCK)
    pad = nb * MOBA_BLOCK - S
    kb = jnp.pad(k, ((0, 0), (0, 0), (0, pad), (0, 0))).reshape(Bn, H, nb, MOBA_BLOCK, dh)
    vb = jnp.pad(v, ((0, 0), (0, 0), (0, pad), (0, 0))).reshape(Bn, H, nb, MOBA_BLOCK, dh)
    k_mean = jnp.mean(kb.astype(jnp.float32), axis=3).astype(q.dtype)
    pos = jnp.arange(S)
    q_blk = pos // MOBA_BLOCK
    gate = jnp.einsum('bhsd,bhnd->bhsn', q, k_mean).astype(jnp.float32)
    past = jnp.arange(nb)[None, :] < q_blk[:, None]
    gate = jnp.where(past, gate, NEG)
    k_sel = min(MOBA_TOPK, nb)
    _, g_idx = lax.top_k(gate, k_sel)
    g_valid = g_idx < q_blk[None, None, :, None]
    scale = dh ** -0.5
    bi = jnp.arange(Bn)[:, None, None, None]
    hi = jnp.arange(H)[None, :, None, None]

    def step(c):
        start = c * MOBA_QCHUNK
        qc = lax.dynamic_slice_in_dim(q, start, MOBA_QCHUNK, axis=2)
        idx = lax.dynamic_slice_in_dim(g_idx, start, MOBA_QCHUNK, axis=2)
        val = lax.dynamic_slice_in_dim(g_valid, start, MOBA_QCHUNK, axis=2)
        blk = start // MOBA_BLOCK
        k_own = lax.dynamic_index_in_dim(kb, blk, axis=2, keepdims=False)
        v_own = lax.dynamic_index_in_dim(vb, blk, axis=2, keepdims=False)
        k_g = kb[bi, hi, idx]
        v_g = vb[bi, hi, idx]
        q_pos = start + jnp.arange(MOBA_QCHUNK)
        k_pos = blk * MOBA_BLOCK + jnp.arange(MOBA_BLOCK)
        s_own = jnp.einsum('bhqd,bhkd->bhqk', qc, k_own).astype(jnp.float32) * scale
        s_own = jnp.where(k_pos[None, :] <= q_pos[:, None], s_own, NEG)
        s_g = jnp.einsum('bhqd,bhqnkd->bhqnk', qc, k_g).astype(jnp.float32) * scale
        s_g = jnp.where(val[..., None], s_g, NEG)
        s = jnp.concatenate([s_own, s_g.reshape(Bn, H, MOBA_QCHUNK, k_sel * MOBA_BLOCK)], axis=-1)
        p = jax.nn.softmax(s, axis=-1).astype(v.dtype)
        p_own = p[..., :MOBA_BLOCK]
        p_g = p[..., MOBA_BLOCK:].reshape(Bn, H, MOBA_QCHUNK, k_sel, MOBA_BLOCK)
        return (jnp.einsum('bhqk,bhkd->bhqd', p_own, v_own)
                + jnp.einsum('bhqnk,bhqnkd->bhqd', p_g, v_g))

    outs = lax.map(step, jnp.arange(S // MOBA_QCHUNK))
    return jnp.moveaxis(outs, 0, 2).reshape(Bn, H, S, dh)

def spatial_gating(u, vg, ln_g, ln_b, w_s, b_s):
    Bn, S, _ = u.shape
    vg = layer_norm(vg, ln_g, ln_b)
    nc = S // SGU_CHUNK
    vr = vg.reshape(Bn, nc, SGU_CHUNK, B_GROUPS, B_DG)
    causal = jnp.tril(jnp.ones((SGU_CHUNK, SGU_CHUNK), dtype=bool))
    w = jnp.where(causal, w_s, jnp.zeros_like(w_s))
    mixed = jnp.einsum('gts,bcsgd->bctgd', w, vr) + b_s.T[None, None, :, :, None]
    return u * mixed.reshape(Bn, S, B_WIDTH)

def mixer_ab(x, w_in, sgu_ln_g, sgu_ln_b, sgu_w, sgu_b, w_out):
    Bn, S, _ = x.shape
    proj = x @ w_in
    qa, ka, va, ub, vb = jnp.split(
        proj, [A_WIDTH, 2 * A_WIDTH, 3 * A_WIDTH, 3 * A_WIDTH + B_WIDTH], axis=-1)
    heads = lambda t: t.reshape(Bn, S, A_HEADS, A_DH).transpose(0, 2, 1, 3)
    pos = jnp.arange(S)
    a = moba_attention(rotary(heads(qa), pos), rotary(heads(ka), pos), heads(va))
    a = a.transpose(0, 2, 1, 3).reshape(Bn, S, A_WIDTH)
    b = spatial_gating(jax.nn.gelu(ub), jax.nn.gelu(vb), sgu_ln_g, sgu_ln_b, sgu_w, sgu_b)
    return jnp.concatenate([a, b], axis=-1) @ w_out

def causal_depthwise_conv(x, w, b):
    K, C = w.shape
    y = lax.conv_general_dilated(x, w[:, None, :], window_strides=(1,), padding=[(K - 1, 0)],
                                 dimension_numbers=('NWC', 'WIO', 'NWC'), feature_group_count=C)
    return y + b

def mlstm_chunkwise(q, k, v, i_pre, f_pre):
    Bn, H, S, dk = q.shape
    dv = v.shape[-1]
    L = MLSTM_CHUNK
    nc = S // L
    f32 = jnp.float32
    qc = q.astype(f32).reshape(Bn, H, nc, L, dk)
    kc = (k.astype(f32) * dk ** -0.5).reshape(Bn, H, nc, L, dk)
    vc = v.astype(f32).reshape(Bn, H, nc, L, dv)
    ic = i_pre.reshape(Bn, H, nc, L)
    b = jnp.cumsum(jax.nn.log_sigmoid(f_pre).reshape(Bn, H, nc, L), axis=-1)
    b_end = b[..., -1]
    a = b_end[..., None] - b + ic
    a_max = jnp.max(a, axis=-1)
    w_end = jnp.exp(a - a_max[..., None])
    kv = jnp.einsum('bhcsk,bhcsv,bhcs->bhckv', kc, vc, w_end)
    ks = jnp.einsum('bhcsk,bhcs->bhck', kc, w_end)

    def scan_fn(carry, inp):
        C, n, m = carry
        kv_c, ks_c, be_c, am_c = inp
        m_new = jnp.maximum(be_c + m, am_c)
        decay = jnp.exp(be_c + m - m_new)
        inject = jnp.exp(am_c - m_new)
        C_new = decay[..., None, None] * C + inject[..., None, None] * kv_c
        n_new = decay[..., None] * n + inject[..., None] * ks_c
        return (C_new, n_new, m_new), (C, n, m)

    init = (jnp.zeros((Bn, H, dk, dv), f32), jnp.zeros((Bn, H, dk), f32), jnp.zeros((Bn, H), f32))
    xs = (jnp.moveaxis(kv, 2, 0), jnp.moveaxis(ks, 2, 0), jnp.moveaxis(b_end, 2, 0), jnp.moveaxis(a_max, 2, 0))
    _, (C_in, n_in, m_in) = lax.scan(scan_fn, init, xs)
    C_in = jnp.moveaxis(C_in, 0, 2)
    n_in = jnp.moveaxis(n_in, 0, 2)
    m_in = jnp.moveaxis(m_in, 0, 2)

    causal = jnp.tril(jnp.ones((L, L), dtype=bool))
    D = b[..., :, None] - b[..., None, :] + ic[..., None, :]
    D = jnp.where(causal, D, -jnp.inf)
    g = b + m_in[..., None]
    m_t = jnp.maximum(g, jnp.max(D, axis=-1))
    P = jnp.exp(D - m_t[..., None])
    sqk = jnp.einsum('bhctk,bhcsk->bhcts', qc, kc) * P
    inter = jnp.exp(g - m_t)
    num = (jnp.einsum('bhcts,bhcsv->bhctv', sqk, vc)
           + inter[..., None] * jnp.einsum('bhctk,bhckv->bhctv', qc, C_in))
    den = jnp.sum(sqk, axis=-1) + inter * jnp.einsum('bhctk,bhck->bhct', qc, n_in)
    h = num / jnp.maximum(jnp.abs(den), jnp.exp(-m_t))[..., None]
    return h.reshape(Bn, H, S, dv)

def mixer_c(x, w_in, conv_w, conv_b, b_i, b_f, head_g, w_out):
    Bn, S, _ = x.shape
    proj = x @ w_in
    qk, v, o_pre, if_pre = jnp.split(
        proj, [2 * C_QK_WIDTH, 2 * C_QK_WIDTH + C_WIDTH, 2 * C_QK_WIDTH + 2 * C_WIDTH], axis=-1)
    qk = jax.nn.silu(causal_depthwise_conv(qk, conv_w, conv_b))
    q, k = jnp.split(qk, 2, axis=-1)
    q = q.reshape(Bn, S, C_HEADS, C_DQK).transpose(0, 2, 1, 3)
    k = k.reshape(Bn, S, C_HEADS, C_DQK).transpose(0, 2, 1, 3)
    v = v.reshape(Bn, S, C_HEADS, C_DV).transpose(0, 2, 1, 3)
    if_f = if_pre.astype(jnp.float32)
    i_pre = (if_f[..., :C_HEADS] + b_i.astype(jnp.float32)).transpose(0, 2, 1)
    f_pre = (if_f[..., C_HEADS:] + b_f.astype(jnp.float32)).transpose(0, 2, 1)
    h = mlstm_chunkwise(q, k, v, i_pre, f_pre)
    mu = jnp.mean(h, axis=-1, keepdims=True)
    var = jnp.mean(jnp.square(h - mu), axis=-1, keepdims=True)
    h = (h - mu) * lax.rsqrt(var + LN_EPS) * head_g.astype(jnp.float32).reshape(C_HEADS, 1, C_DV)
    h = h.transpose(0, 2, 1, 3).reshape(Bn, S, C_WIDTH).astype(x.dtype)
    return (jax.nn.sigmoid(o_pre) * h) @ w_out

def first_inputs(seed: int = 0) -> dict:
    key = jax.random.key(seed)
    ks = jax.random.split(key, 24)
    n_even = (DEPTH + 1) // 2
    n_odd = DEPTH // 2
    nrm = lambda kk, shape, s: s * jax.random.normal(kk, shape, jnp.float32)
    x = nrm(ks[0], (BATCH, SEQ, D_MODEL), 1.0)
    ln_g = 1.0 + nrm(ks[1], (DEPTH, 3, D_MODEL), 0.02)
    ln_b = nrm(ks[2], (DEPTH, 3, D_MODEL), 0.02)
    ffn_w_gu = nrm(ks[3], (DEPTH, 2, D_MODEL, 2 * D_FF), D_MODEL ** -0.5)
    ffn_w_down = nrm(ks[4], (DEPTH, 2, D_FF, D_MODEL), BETA * D_FF ** -0.5)
    ab_cols = jnp.concatenate([jnp.ones((2 * A_WIDTH,), jnp.float32),
                               jnp.full((A_WIDTH,), BETA, jnp.float32),
                               jnp.ones((2 * B_WIDTH,), jnp.float32)])
    ab_w_in = nrm(ks[5], (n_even, D_MODEL, AB_IN), D_MODEL ** -0.5) * ab_cols
    sgu_ln_g = 1.0 + nrm(ks[6], (n_even, B_WIDTH), 0.02)
    sgu_ln_b = nrm(ks[7], (n_even, B_WIDTH), 0.02)
    sgu_w = nrm(ks[8], (n_even, B_GROUPS, SGU_CHUNK, SGU_CHUNK), SGU_CHUNK ** -0.5)
    sgu_b = 1.0 + nrm(ks[9], (n_even, B_GROUPS, SGU_CHUNK), 0.02)
    ab_w_out = nrm(ks[10], (n_even, AB_MIX, D_MODEL), BETA * AB_MIX ** -0.5)
    c_cols = jnp.concatenate([jnp.ones((2 * C_QK_WIDTH,), jnp.float32),
                              jnp.full((C_WIDTH,), BETA, jnp.float32),
                              jnp.ones((C_WIDTH + 2 * C_HEADS,), jnp.float32)])
    c_w_in = nrm(ks[11], (n_odd, D_MODEL, C_IN), D_MODEL ** -0.5) * c_cols
    c_conv_w = nrm(ks[12], (n_odd, CONV_W, 2 * C_QK_WIDTH), CONV_W ** -0.5)
    c_conv_b = nrm(ks[13], (n_odd, 2 * C_QK_WIDTH), 0.02)
    c_b_i = nrm(ks[14], (n_odd, C_HEADS), 0.1)
    c_b_f = jnp.linspace(3.0, 6.0, C_HEADS, dtype=jnp.float32)[None, :] + nrm(ks[15], (n_odd, C_HEADS), 0.1)
    c_head_g = 1.0 + nrm(ks[16], (n_odd, C_WIDTH), 0.02)
    c_w_out = nrm(ks[17], (n_odd, C_WIDTH, D_MODEL), BETA * C_WIDTH ** -0.5)
    return {"x": x, "ln_g": ln_g, "ln_b": ln_b, "ffn_w_gu": ffn_w_gu, "ffn_w_down": ffn_w_down,
            "ab_w_in": ab_w_in, "sgu_ln_g": sgu_ln_g, "sgu_ln_b": sgu_ln_b, "sgu_w": sgu_w,
            "sgu_b": sgu_b, "ab_w_out": ab_w_out, "c_w_in": c_w_in, "c_conv_w": c_conv_w,
            "c_conv_b": c_conv_b, "c_b_i": c_b_i, "c_b_f": c_b_f, "c_head_g": c_head_g,
            "c_w_out": c_w_out}

def first_block(x, ln_g, ln_b, ffn_w_gu, ffn_w_down, ab_w_in, sgu_ln_g, sgu_ln_b, sgu_w, sgu_b,
              ab_w_out, c_w_in, c_conv_w, c_conv_b, c_b_i, c_b_f, c_head_g, c_w_out):
    for l in range(DEPTH):
        x = layer_norm(ALPHA * x + 0.5 * swiglu(x, ffn_w_gu[l, 0], ffn_w_down[l, 0]), ln_g[l, 0], ln_b[l, 0])
        j = l // 2
        if l % 2 == 0:
            y = mixer_ab(x, ab_w_in[j], sgu_ln_g[j], sgu_ln_b[j], sgu_w[j], sgu_b[j], ab_w_out[j])
        else:
            y = mixer_c(x, c_w_in[j], c_conv_w[j], c_conv_b[j], c_b_i[j], c_b_f[j], c_head_g[j], c_w_out[j])
        x = layer_norm(ALPHA * x + y, ln_g[l, 1], ln_b[l, 1])
        x = layer_norm(ALPHA * x + 0.5 * swiglu(x, ffn_w_gu[l, 1], ffn_w_down[l, 1]), ln_g[l, 2], ln_b[l, 2])
    return x


_first_inputs = first_inputs


def first_inputs(seed=0):
    import zlib

    import numpy as np

    out = dict(_first_inputs(seed))
    spreads = {}
    factors = {'sgu_ln_g': 43.716,
     'sgu_ln_b': 44.405,
     'sgu_b': 29.607,
     'c_conv_b': 8.0,
     'c_b_i': 64.0,
     'c_head_g': 25.83}
    for name, (base, spread) in spreads.items():
        noise = np.random.default_rng([zlib.crc32(name.encode()), seed]).standard_normal(out[name].shape)
        drawn = base * np.exp(spread * noise) if base else spread * noise
        out[name] = __import__('jax').numpy.asarray(drawn.astype(out[name].dtype))
    for name, factor in factors.items():
        out[name] = (out[name] * factor).astype(out[name].dtype)
    return out


_narrow_inputs = first_inputs


def first_inputs(seed=0):

    out = dict(_narrow_inputs(seed))
    wider = {'sgu_ln_g': 4.42, 'sgu_ln_b': 4.2, 'sgu_b': 3.91, 'c_head_g': 3.12}
    for name, times in wider.items():
        mean = out[name].mean()
        out[name] = (mean + times * (out[name] - mean)).astype(out[name].dtype)
    return out


HG_HEADS = 4
HG_KDIM = 128
HG_VDIM = 128
HG_CHUNK = 64
ATT_GROUPS = ((128, 1), (512, 4), (2048, 16))
N_GROUPS = 3
ATT_HEADS = 4
ATT_DIM = 128
ROPE_THETA_2 = 500000.0
ROPE_DIM = ATT_DIM // 4
D_FF_2 = 4 * D_MODEL
EPS = 1e-6

HG_QK_W = HG_HEADS * HG_KDIM
HG_V_W = HG_HEADS * HG_VDIM
ATT_W = ATT_HEADS * ATT_DIM
ATT_QKV_W = 3 * N_GROUPS * ATT_W
SPLITS = (HG_QK_W, HG_QK_W, HG_V_W, HG_V_W, ATT_QKV_W, D_MODEL, D_MODEL)
N_IN = HG_QK_W + HG_QK_W + HG_V_W + HG_V_W + ATT_QKV_W + D_MODEL + D_MODEL


def rms_norm(x, g):
    xf = x.astype(jnp.float32)
    y = xf * lax.rsqrt(jnp.mean(xf * xf, axis=-1, keepdims=True) + EPS)
    return (y * g.astype(jnp.float32)).astype(x.dtype)

def partial_rope(t, cos, sin):
    tf = t.astype(jnp.float32)
    c = cos[:, None, :]
    s = sin[:, None, :]
    half = ROPE_DIM // 2
    r1 = tf[..., :half]
    r2 = tf[..., half:ROPE_DIM]
    out = jnp.concatenate([r1 * c - r2 * s, r2 * c + r1 * s, tf[..., ROPE_DIM:]], axis=-1)
    return out.astype(t.dtype)

def hgrn2_chunked(q, log_f, k, v):
    B, S, H, K = q.shape
    V = v.shape[-1]
    C = HG_CHUNK
    nc = S // C

    def chunks(t):
        return t.reshape(B, nc, C, H, t.shape[-1]).swapaxes(0, 1)

    causal = jnp.tril(jnp.ones((C, C), dtype=bool))[None, :, :, None, None]

    def step(state, xs):
        qc, gc, kc, vc = xs
        b = jnp.cumsum(gc, axis=1)
        rel = jnp.where(causal, b[:, :, None] - b[:, None, :], -jnp.inf)
        attn = jnp.einsum('bthk,btshk,bshk->bhts', qc, jnp.exp(rel), kc)
        o = (jnp.einsum('bhts,bshv->bthv', attn, vc)
             + jnp.einsum('bthk,bhkv->bthv', qc * jnp.exp(b), state))
        b_last = b[:, -1]
        k_dec = kc * jnp.exp(b_last[:, None] - b)
        state = state * jnp.exp(b_last)[..., None] + jnp.einsum('bshk,bshv->bhkv', k_dec, vc)
        return state, o

    state0 = jnp.zeros((B, H, K, V), jnp.float32)
    _, o = lax.scan(step, state0, (chunks(q), chunks(log_f), chunks(k), chunks(v)))
    return o.swapaxes(0, 1).reshape(B, S, H, V)

def dilated_window_attention(q, k, v, window, dilation):
    B, S, H, Dh = q.shape
    L = window // dilation
    period = dilation * L
    Sp = -(-S // period) * period
    M = Sp // dilation
    nb = M // L
    pad = Sp - S

    def to_blocks(t):
        t = jnp.pad(t, ((0, 0), (0, pad), (0, 0), (0, 0)))
        t = t.reshape(B, M, dilation, H, Dh)
        t = t.transpose(0, 2, 3, 1, 4)
        return t.reshape(B, dilation, H, nb, L, Dh)

    def with_prev(t):
        prev = jnp.pad(t, ((0, 0), (0, 0), (0, 0), (1, 0), (0, 0), (0, 0)))[:, :, :, :-1]
        return jnp.concatenate([prev, t], axis=4)

    qb = to_blocks(q).astype(jnp.float32)
    kw = with_prev(to_blocks(k)).astype(jnp.float32)
    vw = with_prev(to_blocks(v)).astype(jnp.float32)

    scores = jnp.einsum('bzhnqd,bzhnkd->bzhnqk', qb, kw) * (Dh ** -0.5)
    i = jnp.arange(L)[:, None]
    j = jnp.arange(2 * L)[None, :]
    delta = L + i - j
    band = (delta >= 0) & (delta <= L)
    n = jnp.arange(nb)[:, None, None]
    mask = band[None] & ((n > 0) | (j[None] >= L))
    scores = jnp.where(mask, scores, -jnp.inf)
    m = jnp.max(scores, axis=-1, keepdims=True)
    p = jnp.exp(scores - m)
    den = jnp.sum(p, axis=-1, keepdims=True)
    o = jnp.einsum('bzhnqk,bzhnkd->bzhnqd', p, vw) / den
    lse = (m + jnp.log(den))[..., 0]

    o = o.reshape(B, dilation, H, M, Dh).transpose(0, 3, 1, 2, 4).reshape(B, Sp, H, Dh)[:, :S]
    lse = lse.reshape(B, dilation, H, M).transpose(0, 3, 1, 2).reshape(B, Sp, H)[:, :S]
    return o, lse

def second_inputs(seed: int = 0) -> dict:
    key = jax.random.key(seed)
    ks = jax.random.split(key, 13)
    f32 = jnp.float32
    nrm = lambda k, shape, scale: jax.random.normal(k, shape, f32) * scale
    return {
        "x": nrm(ks[0], (BATCH, SEQ, D_MODEL), 1.0),
        "norm1_g": 1.0 + nrm(ks[1], (DEPTH, D_MODEL), 0.02),
        "w_in": nrm(ks[2], (DEPTH, D_MODEL, N_IN), D_MODEL ** -0.5),
        "hg_lower_bounds": nrm(ks[3], (DEPTH, HG_QK_W), 1.0),
        "hg_norm_g": 1.0 + nrm(ks[4], (DEPTH, HG_V_W), 0.02),
        "w_branch_a": nrm(ks[5], (DEPTH, HG_V_W, D_MODEL), HG_V_W ** -0.5),
        "w_branch_b": nrm(ks[6], (DEPTH, ATT_W, D_MODEL), ATT_W ** -0.5),
        "w_out": nrm(ks[7], (DEPTH, D_MODEL, D_MODEL), D_MODEL ** -0.5),
        "norm2_g": 1.0 + nrm(ks[8], (DEPTH, D_MODEL), 0.02),
        "w_up": nrm(ks[9], (DEPTH, D_MODEL, D_FF_2), D_MODEL ** -0.5),
        "w_down": nrm(ks[10], (DEPTH, D_FF_2, D_MODEL), D_FF_2 ** -0.5),
        "final_norm_g": 1.0 + nrm(ks[11], (D_MODEL,), 0.02),
    }

def second_block(x, norm1_g, w_in, hg_lower_bounds, hg_norm_g, w_branch_a, w_branch_b,
              w_out, norm2_g, w_up, w_down, final_norm_g):
    B, S, _ = x.shape
    f32 = jnp.float32
    split_idx = [int(c) for c in np.cumsum(SPLITS)[:-1]]

    pos = jnp.arange(S, dtype=f32)
    inv_freq = ROPE_THETA_2 ** (-jnp.arange(0, ROPE_DIM, 2, dtype=f32) / ROPE_DIM)
    ang = pos[:, None] * inv_freq[None, :]
    cos, sin = jnp.cos(ang), jnp.sin(ang)

    lb_all = jnp.cumsum(jax.nn.softmax(hg_lower_bounds.astype(f32), axis=0), axis=0)
    lb_all = lb_all - lb_all[0:1]

    for l in range(DEPTH):
        h = rms_norm(x, norm1_g[l])
        z = h @ w_in[l]
        zq, zf, zi, zg, zatt, za, zb = jnp.split(z, split_idx, axis=-1)

        q_hg = jax.nn.silu(zq.astype(f32)).reshape(B, S, HG_HEADS, HG_KDIM)
        lb = lb_all[l]
        log_f = jnp.logaddexp(jnp.log(lb), jnp.log1p(-lb) + jax.nn.log_sigmoid(zf.astype(f32)))
        log_f = log_f.reshape(B, S, HG_HEADS, HG_KDIM)
        k_hg = -jnp.expm1(log_f)
        v_hg = zi.astype(f32).reshape(B, S, HG_HEADS, HG_VDIM)
        o_hg = hgrn2_chunked(q_hg, log_f, k_hg, v_hg)
        o_hg = rms_norm(o_hg, hg_norm_g[l].reshape(HG_HEADS, HG_VDIM))
        o_hg = o_hg * jax.nn.sigmoid(zg.astype(f32)).reshape(B, S, HG_HEADS, HG_VDIM)
        o_hg = o_hg.reshape(B, S, HG_V_W).astype(x.dtype)

        qkv = zatt.reshape(B, S, 3, N_GROUPS, ATT_HEADS, ATT_DIM)
        outs, lses = [], []
        for g, (window, dilation) in enumerate(ATT_GROUPS):
            qg = partial_rope(qkv[:, :, 0, g], cos, sin)
            kg = partial_rope(qkv[:, :, 1, g], cos, sin)
            vg = qkv[:, :, 2, g]
            o_g, lse_g = dilated_window_attention(qg, kg, vg, window, dilation)
            outs.append(o_g)
            lses.append(lse_g)
        w_grp = jax.nn.softmax(jnp.stack(lses, axis=0), axis=0)
        o_att = jnp.sum(w_grp[..., None] * jnp.stack(outs, axis=0), axis=0)
        o_att = o_att.reshape(B, S, ATT_W).astype(x.dtype)

        y = (jax.nn.sigmoid(za) * (o_hg @ w_branch_a[l])
             + jax.nn.sigmoid(zb) * (o_att @ w_branch_b[l]))
        x = x + y @ w_out[l]

        h2 = rms_norm(x, norm2_g[l])
        x = x + jnp.square(jax.nn.relu(h2 @ w_up[l])) @ w_down[l]

    return rms_norm(x, final_norm_g)


def setup_inputs(seed=0):
    out = dict(first_inputs(seed))
    for name, value in second_inputs(seed + 1).items():
        if name != "x":
            out[name + "_2"] = value
    return out


def reference(
    x, ln_g, ln_b, ffn_w_gu, ffn_w_down, ab_w_in, sgu_ln_g, sgu_ln_b, sgu_w, sgu_b, ab_w_out,
    c_w_in, c_conv_w, c_conv_b, c_b_i, c_b_f, c_head_g, c_w_out, norm1_g_2, w_in_2,
    hg_lower_bounds_2, hg_norm_g_2, w_branch_a_2, w_branch_b_2, w_out_2, norm2_g_2, w_up_2,
    w_down_2, final_norm_g_2,
):
    x = first_block(
        x, ln_g, ln_b, ffn_w_gu, ffn_w_down, ab_w_in, sgu_ln_g, sgu_ln_b, sgu_w, sgu_b,
        ab_w_out, c_w_in, c_conv_w, c_conv_b, c_b_i, c_b_f, c_head_g, c_w_out,
    )
    return second_block(
        x, norm1_g_2, w_in_2, hg_lower_bounds_2, hg_norm_g_2, w_branch_a_2, w_branch_b_2,
        w_out_2, norm2_g_2, w_up_2, w_down_2, final_norm_g_2,
    )


_drawn_inputs = setup_inputs


def setup_inputs(seed=0):
    import zlib

    import numpy as np

    out = dict(_drawn_inputs(seed))
    spreads = {}
    factors = {'norm1_g_2': 4.657, 'hg_lower_bounds_2': 23.707, 'hg_norm_g_2': 7.753, 'norm2_g_2': 3.144}
    for name, (base, spread) in spreads.items():
        noise = np.random.default_rng([zlib.crc32(name.encode()), seed]).standard_normal(out[name].shape)
        drawn = base * np.exp(spread * noise) if base else spread * noise
        out[name] = __import__('jax').numpy.asarray(drawn.astype(out[name].dtype))
    for name, factor in factors.items():
        out[name] = (out[name] * factor).astype(out[name].dtype)
    return out
```

```python
from contextlib import ExitStack

import concourse.bass as bass
import numpy as np
from concourse import mybir

ALU = mybir.AluOpType
ACT = mybir.ActivationFunctionType
AX = mybir.AxisListType.X
F32 = mybir.dt.float32
F32R = mybir.dt.float32r
I32 = mybir.dt.int32

P = 128
S = 256
TT = S // P
D = 1024
DT = D // P
CH = 512
BK = 2
RAW = 8
SPLIT = 4
AUX = 4
DEPTH = 2
ALPHA = (2 * DEPTH) ** 0.25
LN_EPS = 1e-5
RMS_EPS = 1e-6
NEG = -1e30
LEVELS = 7
CHUNK = 64
F_MIN = 1e-19


CONST_COLS = {}


def constant_tables():
    parts = []

    def put(name, a):
        a = np.asarray(a, np.float32)
        full = np.zeros((P, a.shape[1]), np.float32)
        full[: a.shape[0]] = a
        start = sum(x.shape[1] for x in parts)
        CONST_COLS[name] = (start, start + a.shape[1])
        parts.append(full)

    i = np.arange(P)
    put("ident", np.eye(P))
    put("swap_a", np.eye(P)[(i // 64) * 64 + (i % 64 + 32) % 64])
    pos = np.arange(S, dtype=np.float32)

    def rope(half, theta_powers, width):
        ang = pos[None, :] * theta_powers[np.arange(width) % half][:, None]
        sign = np.where(np.arange(width) % (2 * half) < half, -1.0, 1.0)[:, None]
        return np.cos(ang), np.sin(ang) * sign

    inv_a = (np.float32(10000.0) ** (-np.arange(32, dtype=np.float32) / np.float32(32))).astype(np.float32)
    inv_b = (np.float32(500000.0) ** (-np.arange(0, 32, 2, dtype=np.float32) / np.float32(32))).astype(np.float32)
    for tag, half, inv, width in (("a", 32, inv_a, P), ("b", 16, inv_b, 32)):
        c, s = rope(half, inv, width)
        put("cos_" + tag, c)
        put("sin_" + tag, s)
    t, s = i[:, None], i[None, :]
    add = lambda keep: np.where(keep, 0.0, NEG)
    put("causal_key_major", add(t <= s))
    put("zeros", np.zeros((P, P)))
    put("causal", add(s <= t))
    for d in (1, 4, 16):
        back = P + t - s
        put(f"before_{d}", add((back % d == 0) & (back <= P * d)))
        put(f"own_{d}", add((s <= t) & ((t - s) % d == 0)))
    put("upper", t <= s)
    put("ones", np.ones((P, 64)))
    put("pick_head", np.repeat(np.eye(4), P, axis=1))
    levels = []
    for l in range(1, LEVELS + 1):
        w = 2 ** l
        levels.append((t // w == s // w) & (t % w < w // 2) & (s % w >= w // 2))
    return np.concatenate(parts, axis=1), np.concatenate(levels, axis=1).astype(np.float32)


constant_tables()

D_FF = 2816
FF1 = D_FF
FF1_TILES = {5: (0, 2)} | {c: (2 + 4 * (c - 6), 4) for c in range(6, 11)}
PARAM_ROWS = 64
CONST_WIDTH = max(b for _, b in CONST_COLS.values())


HEADS_A, DH_A = 8, 64
HEADS_C, DQK_C, DV_C = 4, 128, 256
HEADS_G = 4
GROUPS = 3
CONV_W_AT, CONV_B_AT, HEAD_G_AT, BOUND_AT, HG_NORM_AT = 0, 32, 40, 48, 56


def tiles_of(bank, n):
    return bank[:, 0:n * P].rearrange("p (k t) -> p k t", t=P)


class Seen:

    def __getattr__(self, name):
        if name.startswith("__"):
            raise AttributeError(name)
        return 0


class Norm:
    def __init__(self, kind, rows, turned=True):
        self.kind, self.rows, self.turned = kind, rows, turned
        self.eps = LN_EPS if kind == "ln" else RMS_EPS


class Stage:
    def __init__(self, kind, lins, norms, layer=0):
        self.kind, self.lins, self.norms, self.layer = kind, lins, norms, layer


def LINS(stages):
    return [lin for st in stages for lin in st.lins]


def all_stages(io):
    out = []
    ln = lambda l, i, **kw: Norm("ln", [io["ln_g"][l, i:i + 1], io["ln_b"][l, i:i + 1]], **kw)
    rms = lambda g, **kw: Norm("rms", [g], **kw)
    for l in range(DEPTH):
        for i in range(2):
            up = Linear(io["ffn_w_gu"][l, i], D, 2 * D_FF)
            down = Linear(io["ffn_w_down"][l, i], D_FF, D)
            last = l == DEPTH - 1 and i == 1
            norms = [ln(l, 2 * i, turned=not last)]
            if last:
                norms.append(rms(io["norm1_g_2"][0:1]))
            out.append(Stage("ffn1", [up, down], norms, l))
            if i == 0:
                if l == 0:
                    lins = [Linear(io["ab_w_in"][0], D, 2560, (2, 0, 1, 4, 3)), Linear(io["ab_w_out"][0], D, D)]
                else:
                    lins = [Linear(io["c_w_in"][0], D, 3072, (2, 0, 1)), Linear(io["c_w_out"][0], D, D)]
                out.append(Stage("ab" if l == 0 else "c", lins, [ln(l, 1)], l))
    for l in range(DEPTH):
        lins = [Linear(io["w_in_2"][l], D, 8704, (2, 1, 0)), Linear(io["w_branch_a_2"][l], 512, D),
                Linear(io["w_branch_b_2"][l], 512, D), Linear(io["w_out_2"][l], D, D)]
        out.append(Stage("hg", lins, [rms(io["norm2_g_2"][l:l + 1])], l))
        g = io["norm1_g_2"][l + 1:l + 2] if l + 1 < DEPTH else io["final_norm_g_2"].rearrange("(a d) -> a d", a=1)
        lins = [Linear(io["w_up_2"][l], D, 4 * D), Linear(io["w_down_2"][l], 4 * D, D)]
        out.append(Stage("ffn2", lins, [rms(g, turned=l + 1 < DEPTH)], l))
    return out

class Batch:

    def __init__(self, tt, heads, groups):
        self.tt, self.heads, self.groups = tt, heads, groups
        self.keys = (tt + 1) * P
        self.width = self.keys * len(heads) * groups
        self.segments = len(heads)
        self.pieces = [(h, g, kt) for h in heads for g in range(groups) for kt in range(tt + 1)]
        self.banks = -(-self.width // CH)

    def bank_width(self, i):
        return min(CH, self.width - i * CH)


BATCHES_A = [Batch(0, range(h, 8, 2), 1) for h in (0, 1)] + \
    [Batch(1, range(h, h + 4, 2), 1) for h in (0, 4, 1, 5)]
BATCHES_G = [Batch(tt, [h], GROUPS) for tt in range(TT) for h in range(HEADS_G)]


def step_at(lin, c, j, first):
    step = first + (c * lin.kb + j) // 2
    return step if 0 <= step < len(BATCHES_G) + 2 else None



class At:

    def __init__(self, like, turn=0):
        self.like, self.turn = like, turn
        self.c = like + 2 * turn


def chunks(eng, lo, hi, body, peel=0):
    for c in range(lo, min(hi, lo + peel)):
        body(At(c))
    lo = min(hi, lo + peel)
    pairs = (hi - lo) // 2
    if pairs >= 2:
        with eng.Fori(0, pairs) as turn:
            for c in (lo, lo + 1):
                body(At(c, turn))
        lo += 2 * pairs
    for c in range(lo, hi):
        body(At(c))


class Linear:

    def __init__(self, w, k, n, order=()):
        self.order = order
        self.w, self.kb, self.n = w, k // (P * BK), n // CH
        self.b0 = self.c0 = 0
        self.early = False

    def block(self, at, j):
        return self.b0 + at.like * self.kb + j, at.turn * 2 * self.kb

    def columns(self, at):
        return bass.ds((self.order[at.like] if at.like < len(self.order) else at.c) * CH, CH)

    def chunk(self, at):
        return self.c0 + at.c

    def banks(self, at):
        return 2 * ((self.c0 + at.like) % 2)

    def done(self, at):
        b, turn = self.block(at, self.kb - 1)
        return b + turn + 1


class Steps:

    def __init__(self, eng, sem):
        self.eng, self.sem, self.n = eng, sem, 0

    def __call__(self, *instructions):
        for ins in instructions:
            self.n += 1
            ins.then_inc(self.sem, 1)
        self.eng.wait_ge(self.sem, self.n)


def program(nc, io, out, stages):
    ctx = ExitStack()
    with ctx:
        def sem(name):
            return ctx.enter_context(nc.semaphore(name))

        base = (nc.sbuf_base + 63) // 64 * 64
        top = [base]

        def sb(name, shape, dtype=F32, at=None):
            size = int(np.prod(shape[1:])) * mybir.dt.size(dtype)
            where = top[0] if at is None else arena + at
            if at is None:
                top[0] += (size + 63) // 64 * 64
            assert where + size <= nc.sbuf_usable_end, (name, where + size, nc.sbuf_usable_end)
            return nc.alloc_sbuf_tensor_at(name, shape, dtype, offset=where)

        KB = 1024
        raw = sb("raw", [P, RAW, BK, CH])
        whi = sb("whi", [P, SPLIT, BK, CH], F32R)
        wlo = sb("wlo", [P, SPLIT, BK, CH], F32R)
        x = sb("x", [P, TT, D])
        xhi = sb("xhi", [P, DT, S], F32R)
        xlo = sb("xlo", [P, DT, S], F32R)
        gain = sb("gain", [P, 2, D])
        const = sb("const", [P, CONST_WIDTH])
        level_mask = sb("level_mask", [P, LEVELS, P])
        params = sb("params", [P, PARAM_ROWS])
        stats = sb("stats", [P, 2, TT, 4, 6])
        moments = sb("moments", [P, TT, 4, 2])
        spread = sb("spread", [P, TT, 4])
        deviation = sb("deviation", [P, TT, 4])
        small = sb("small", [P, 64])
        param_rows = sb("param_rows", [PARAM_ROWS, P])
        gate_bias = sb("gate_bias", [HEADS_C, 2])
        bound = sb("bound", [P, 2, HEADS_G])
        arena = top[0]
        hhi = sb("hhi", [P, 32, S], F32R, at=0)
        hlo = sb("hlo", [P, 32, S], F32R, at=32 * KB)
        silu_gate = sb("silu_gate", [P, TT, FF1], at=56 * KB)
        up_part = [sb(f"up_part{i}", [P, TT, CH], at=56 * KB + TT * FF1 * 4 + i * 4 * KB) for i in range(2)]
        relu_part = [sb(f"relu_part{i}", [P, TT, CH], at=(64 + 4 * i) * KB) for i in range(2)]
        y = sb("y", [P, TT, D], at=72 * KB)
        normed = y
        early_hi = sb("early_hi", [P, SPLIT, BK, CH], F32R, at=56 * KB)
        early_lo = [sb(f"early_lo{i}", [P, 2, BK, CH], F32R, at=at * KB) for i, at in enumerate((22, 80))]
        gain_more = sb("gain_more", [P, D], at=90 * KB)

        qa = sb("qa", [P, 4, S], at=8 * KB)
        ka = sb("ka", [P, 4, S], at=12 * KB)
        va = sb("va", [P, TT, CH], at=16 * KB)
        ua = sb("ua", [P, 4, S], at=20 * KB)
        rope_scratch = sb("rope_scratch", [P, D], at=90 * KB)
        att = [sb(f"att{i}", [P, 6 * P], at=(24 + 3 * i) * KB) for i in range(2)]
        att_t = [sb(f"att_t{i}", [P, 6 * P], at=(40 + 3 * i) * KB) for i in range(2)]
        vgate = sb("vgate", [P, TT, CH], at=46 * KB)
        sgu_wt = sb("sgu_wt", [P, 8, P], at=50 * KB)
        sgu_w = sb("sgu_w", [P, 8, P], at=54 * KB)
        sgu_gain = sb("sgu_gain", [P, 2, CH], at=58 * KB)
        sgu_bias = sb("sgu_bias", [1, 8 * P], at=62 * KB)
        gated = [sb(f"gated{i}", [P, CH], at=(66 + 2 * i) * KB) for i in range(2)]
        conv_in = sb("conv_in", [P, 8, S + 3], at=8 * KB)
        conv = sb("conv", [P, 8, S], at=17 * KB)
        (in_row, forget_row, sum_row, max_row, unit_row, zero_row) = (
            sb(name, [HEADS_C, S], at=(25 + i) * KB)
            for i, name in enumerate(("in_row", "forget_row", "sum_row", "max_row", "unit_row", "zero_row")))
        gate_w = sb("gate_w", [P, DT, 8], at=31 * KB)
        gate_tok = sb("gate_tok", [P, 16], at=31 * KB + 256)
        gate_cols = sb("gate_cols", [P, 16], at=31 * KB + 320)
        vc = sb("vc", [P, TT, HEADS_C, DV_C + 1], at=40 * KB)
        out_gate = sb("out_gate", [P, 8, S], at=49 * KB)
        heads_out = sb("heads_out", [P, TT, D], at=57 * KB)
        mix_w = [sb(f"mix_w{i}", [P, 3 * P], at=65 * KB + i * 1536) for i in range(2)]
        gated_c = [sb(f"gated_c{i}", [P, CH], at=(68 + 2 * i) * KB) for i in range(2)]
        hq = sb("hq", [P, 4, S], at=8 * KB)
        hk = sb("hk", [P, 4, S], at=12 * KB)
        hv = sb("hv", [P, TT, CH], at=16 * KB)
        hgate = sb("hgate", [P, TT, CH], at=20 * KB)
        decay_sum = sb("decay_sum", [P, 4, S], at=24 * KB)
        decayed = [sb("decayed0", [P, 4, S], at=28 * KB), sb("decayed1", [P, 4, S], at=40 * KB)]
        pair_w = sb("pair_w", [P, 3, CH], at=44 * KB)
        rope_swap = [sb(f"rope_swap{i}", [32, 4, S], at=(86 + 4 * i) * KB) for i in range(2)]
        o_hg = sb("o_hg", [P, TT, CH], at=86 * KB)
        o_square = sb("o_square", [P, TT, CH], at=90 * KB)
        aq = sb("aq", [P, 12, S], at=50 * KB)
        ak = sb("ak", [P, 12, S], at=62 * KB)
        av = sb("av", [P, GROUPS, TT, CH], at=74 * KB)
        gate_a = sb("gate_a", [P, TT, D], at=8 * KB)
        gate_b = sb("gate_b", [P, TT, D], at=16 * KB)
        branch_a = sb("branch_a", [P, TT, D], at=86 * KB)
        branch_b = sb("branch_b", [P, TT, D], at=50 * KB)

        stream = [ctx.enter_context(nc.psum_tensor(f"stream{i}", [P, CH], F32)) for i in range(4)]
        aux = [ctx.enter_context(nc.psum_tensor(f"aux{i}", [P, CH], F32)) for i in range(AUX)]

        def cst(name, rows=P):
            a, b = CONST_COLS[name]
            return const[0:rows, a:b]

        ident = cst("ident")

        raw_in = [sem(f"raw_in{i}") for i in range(RAW)]
        hi_ready = sem("hi_ready")
        lo_ready = sem("lo_ready")
        block_used = sem("block_used")
        evicted = sem("evicted")
        aux_full = sem("aux_full")
        aux_hi = sem("aux_hi")
        aux_free = sem("aux_free")
        h_made = sem("h_made")
        x_summed = sem("x_summed")
        tile_done = sem("tile_done")
        x_normed = sem("x_normed")
        var_ready = sem("var_ready")
        std_ready = sem("std_ready")
        ident_in = sem("ident_in")
        const_in = sem("const_in")
        gain_in = sem("gain_in")
        gain_used = sem("gain_used")
        x_in = [sem(f"x_in{tt}") for tt in range(TT)]
        out_in = sem("out_in")
        param_in = sem("param_in")
        side_in = sem("side_in")
        roped = sem("roped")
        swap_in = [sem(f"swap_in{i}") for i in range(2)]
        logits_ready = sem("logits_ready")
        exps_ready = sem("exps_ready")
        totals_ready = sem("totals_ready")
        scaled = sem("scaled")
        probs_ready = sem("probs_ready")
        vgate_normed = sem("vgate_normed")
        mixed_full = sem("mixed_full")
        gated_ready = sem("gated_ready")
        mixed_hi = sem("mixed_hi")
        mixed_lo = sem("mixed_lo")
        rows_ready = sem("rows_ready")
        rows_exp = sem("rows_exp")
        gates_copied = sem("gates_copied")
        conv_done = sem("conv_done")
        conv_silu = sem("conv_silu")
        decay_arg = sem("decay_arg")
        decay_exp = sem("decay_exp")
        decay_used = sem("decay_used")
        heads_normed = sem("heads_normed")
        bound_arg = sem("bound_arg")
        bound_exp = sem("bound_exp")
        f_ready = sem("f_ready")
        logf_ready = sem("logf_ready")
        pairs_ready = sem("pairs_ready")
        act_step = sem("act_step")
        dve_step = sem("dve_step")

        for before, lin in zip([None, *LINS(stages)], LINS(stages)):
            if before is not None:
                lin.b0 = before.b0 + before.n * before.kb
                lin.c0 = before.c0 + before.n
        lins = LINS(stages)
        for before, st in zip(stages, stages[1:]):
            st.lins[0].early = before.kind != "ffn2"

        place = {}
        for before, st in zip(stages, stages[1:]):
            b = st.lins[0].b0
            if before.kind == "ffn1":
                for n, block in enumerate((b, b + 1, b - 3, b + 2, b + 3, b - 2, b - 1)):
                    place[block] = b - 3 + n

        def split_count(b, turn=0):
            return place.get(b, b) + turn + 1

        def split_slots(lin, at, j):
            if lin.early and at.like == 0:
                return early_hi[:, j], early_lo[j // 2][:, j % 2]
            slot = lin.block(at, j)[0] % SPLIT
            return whi[:, slot], wlo[:, slot]

        for before, st in zip([None, *stages], stages):
            st.gain_at = (before.gain_at if before else 0) + 16 * sum(len(norm.rows) for norm in st.norms)
            at = 0
            for norm in st.norms:
                norm.gain = [gain[:, at + i] if at + i < 2 else gain_more[:] for i in range(len(norm.rows))]
                at += len(norm.rows)

        def following(lin):
            i = lins.index(lin) + 1
            return lins[i] if i < len(lins) else None

        def last_chunk(lin, split, j0=0, early=SPLIT):
            after = following(lin)
            if after is None or not after.early:
                split(lin, At(1), j0)
            elif after.b0 in place:
                split(lin, At(1), j0, lin.kb - 3)
                split(after, At(0), 0, 2)
                split(lin, At(1), lin.kb - 3, lin.kb - 2)
                split(after, At(0), 2, 4)
                split(lin, At(1), lin.kb - 2)
            else:
                split(lin, At(1), j0)
                split(after, At(0), 0, early)

        def preceding(lin):
            return lins[lins.index(lin) - 1]

        block = ctx.enter_context(nc.Block())

        @block.sync
        def _(sp):
            sp.dma_start(ident, io["const"][:, 0:P]).then_inc(ident_in, 16)
            def load_x(tt):
                sp.dma_start(x[:, tt], io["x"][0, tt * P:(tt + 1) * P]).then_inc(x_in[tt], 16)

            load_x(0)

            def load(lin, at):
                for j in range(lin.kb):
                    b, turn = lin.block(at, j)
                    slot = b % RAW
                    if b >= RAW:
                        sp.wait_ge(lo_ready, split_count(b - RAW, turn))
                    src = lin.w[j * BK * P:(j + 1) * BK * P, lin.columns(at)]
                    sp.dma_start(raw[:, slot], src.rearrange("(k p) n -> p k n", p=P)).then_inc(raw_in[slot], 16)
                    if lin is lins[0] and at.like == 0 and j == SPLIT - 2:
                        load_x(1)

            for lin in lins:
                chunks(sp, 0, lin.n, lambda at: load(lin, at), peel=4 if lin.b0 in place else max(len(lin.order), 2))
            for tt in range(TT):
                sp.wait_ge(x_normed, 2 * TT * (len(stages) - 1) + 2 * tt + 2)
                sp.dma_start(out[0, tt * P:(tt + 1) * P, :], normed[:, tt]).then_inc(out_in, 16)
            sp.wait_ge(out_in, 16 * TT)

        @block.gpsimd
        def _(pool):
            def side(st):
                if st.kind not in ("ab", "c"):
                    return
                if st.lins[0].b0:
                    pool.wait_ge(block_used, st.lins[0].b0 + st.lins[0].kb)
                if st.kind == "ab":
                    pool.dma_start(sgu_w[:], io["sgu_w"][0].rearrange("g t s -> t g s")).then_inc(side_in, 16)
                    for i, name in enumerate(("sgu_ln_g", "sgu_ln_b")):
                        pool.dma_start(sgu_gain[:, i], io[name].partition_broadcast(P)).then_inc(side_in, 16)
                    pool.dma_start(sgu_bias[:], io["sgu_b"].rearrange("a g t -> a (g t)")).then_inc(side_in, 16)
                else:
                    gates = io["c_w_in"][0][:, 3 * D:3 * D + 8].rearrange("(k p) n -> p k n", p=P)
                    pool.dma_start(gate_w[:], gates).then_inc(side_in, 16)

            pool.wait_ge(raw_in[3], 16)
            pool.dma_start(const[:, P:], io["const"][:, P:]).then_inc(const_in, 16)
            pool.dma_start(level_mask[:], io["level_mask"].rearrange("p (l t) -> p l t", t=P)).then_inc(const_in, 16)
            for at, name, pattern in (
                    (CONV_W_AT, "c_conv_w", "a j (t p) -> (a j t) p"), (CONV_B_AT, "c_conv_b", "a (t p) -> (a t) p"),
                    (HEAD_G_AT, "c_head_g", "a (t p) -> (a t) p"),
                    (BOUND_AT, "hg_lower_bounds_2", "a (t p) -> (a t) p"),
                    (HG_NORM_AT, "hg_norm_g_2", "a (t p) -> (a t) p")):
                src = io[name].rearrange(pattern, p=P)
                pool.dma_start(param_rows[at:at + src.shape[0], :], src).then_inc(param_in, 16)
            for i, name in enumerate(("c_b_i", "c_b_f")):
                pool.dma_start(gate_bias[:, i:i + 1], io[name].rearrange("a h -> h a")).then_inc(param_in, 16)
            seen = Seen()

            def swaps(st):
                for c in range(5, 11):
                    tiles = (aq if c < 8 else ak)[:, 4 * ((c - 5) % 3):4 * ((c - 5) % 3) + 4]
                    pool.wait_ge(evicted, 2 * (st.lins[0].c0 + c - 1) + 2)
                    if seen.roped >= 2:
                        pool.wait_ge(roped, seen.roped - 1 + seen.rotated)
                    seen.roped += 1
                    for to, half in ((0, 16), (16, 0)):
                        pool.dma_start(rope_swap[c % 2][to:to + 16], tiles[half:half + 16]).then_inc(swap_in[c % 2], 16)

            for n, st in enumerate(stages):
                side(st)
                if n:
                    pool.wait_ge(gain_used, n)
                for norm in st.norms:
                    for to, row in zip(norm.gain, norm.rows):
                        pool.dma_start(to, row.partition_broadcast(P)).then_inc(gain_in, 16)
                if st.kind == "ab":
                    seen.rotated += 2
                if st.kind == "hg":
                    swaps(st)

        @block.scalar
        def _(act):
            step = Steps(act, act_step)
            seen = Seen()

            def split(lin, at, j0=0, j1=None):
                for j in range(j0, lin.kb if j1 is None else j1):
                    b, turn = lin.block(at, j)
                    act.wait_ge(raw_in[b % RAW], 16 * (b // RAW + 1) + 16 * at.turn * (2 * lin.kb // RAW))
                    if lin.early and at.like == 0:
                        act.wait_ge(block_used, lin.b0 - preceding(lin).kb)
                    elif b >= SPLIT:
                        act.wait_ge(block_used, b + turn - SPLIT + 1)
                    act.activation(split_slots(lin, at, j)[0], raw[:, b % RAW], ACT.Copy).then_inc(hi_ready, 1)

            def ahead(lin):
                if lin is not None:
                    split(lin, At(0), 0, min(lin.kb, SPLIT))

            def evict(lin, at, dst, func=ACT.Copy):
                act.wait_ge(block_used, lin.done(at))
                for i in range(2):
                    act.activation(dst(i), stream[lin.banks(at) + i][:], func).then_inc(evicted, 1)

            def last_layer(lin, j0=0):
                split(lin, At(0), j0)
                last_chunk(lin, split)

            def layer(lin, place, func=lambda c: ACT.Copy, after=lambda c: None, within=lambda c, j: None):
                for c in range(lin.n):
                    to, at = (lin, At(c + 1)) if c + 1 < lin.n else (following(lin), At(0))
                    for j in range(max(lin.kb, to.kb)):
                        within(c, j)
                        if j < to.kb:
                            split(to, at, j, j + 1)
                    if place(c) is not None:
                        evict(lin, At(c), place(c), func(c))
                    after(c)

            def turn_hi(dst, n, more=0):
                act.wait_ge(aux_full, seen.aux + 1 + more)
                act.activation(dst, tiles_of(aux[seen.aux % AUX], n), ACT.Copy).then_inc(aux_hi, 1)
                seen.aux += 1

            def root(*where):
                seen.var += 1
                act.wait_ge(var_ready, seen.var)
                act.activation(deviation[where], spread[where], ACT.Sqrt).then_inc(std_ready, 1)

            def norm_act(st):
                lin = following(st.lins[-1])
                turned = st.norms[-1].turned

                def ahead(j):
                    if lin is not None and not lin.early:
                        split(lin, At(0), j, j + 1)

                def x_turn_hi(tt, half):
                    if turned:
                        turn_hi(xhi[:, half * 4:half * 4 + 4, tt * P:(tt + 1) * P], 4)

                for _ in st.norms:
                    root(slice(None), 0, slice(0, 1))
                ahead(0)
                ahead(1)
                ahead(2)
                x_turn_hi(0, 0)
                ahead(3)
                x_turn_hi(0, 1)
                for _ in st.norms:
                    root(slice(None), 1, slice(0, 1))
                x_turn_hi(1, 0)
                x_turn_hi(1, 1)

            def h_turn_hi(first_tile, tiles):
                for tt in range(TT):
                    turn_hi(hhi[:, first_tile:first_tile + tiles, tt * P:(tt + 1) * P], tiles)

            def ffn1(st):
                up, down = st.lins
                split(up, At(0), SPLIT)

                def gate(at):
                    split(up, At(at.like + 1, at.turn))
                    evict(up, at, lambda tt: silu_gate[:, tt, bass.ds(at.c * CH, CH)], ACT.Silu)

                chunks(act, 0, 5, gate, peel=1)
                if st is stages[0]:
                    seen.aux += 1
                split(up, At(6))
                act.wait_ge(block_used, up.done(At(5)))
                for tt in range(TT):
                    bank = stream[up.banks(At(5)) + tt]
                    act.activation(silu_gate[:, tt, 5 * CH:FF1], bank[:, 0:CH // 2], ACT.Silu)
                    act.activation(up_part[1][:, tt, CH // 2:CH], bank[:, CH // 2:CH], ACT.Copy).then_inc(evicted, 1)
                h0 = seen.h
                for c in range(6, up.n):
                    if c + 1 < up.n:
                        split(up, At(c + 1))
                    else:
                        ahead(down)
                    if c > 6:
                        act.wait_ge(h_made, h0 + c - 6)
                    evict(up, At(c), lambda tt: up_part[c % 2][:, tt, :])
                    h_turn_hi(*FF1_TILES[c - 1])
                split(down, At(0), SPLIT, SPLIT + 2)
                h_turn_hi(*FF1_TILES[up.n - 1])
                last_layer(down, SPLIT + 2)
                seen.h += 6

            def attention(batches, between):
                for n, batch in enumerate(batches):
                    seen.logits += 1
                    act.wait_ge(logits_ready, seen.logits)
                    w = batch.width // batch.segments
                    for i in range(batch.segments):
                        part = att[n % 2][:, i * w:(i + 1) * w]
                        low, total = small[:, 4 * (n % 2) + i:4 * (n % 2) + i + 1], small[:, 8 + 4 * (n % 2) + i:9 + 4 * (n % 2) + i]
                        e = act.activation(part, part, ACT.Exp, bias=low, accum_out=total)
                    e.then_inc(exps_ready, 1)
                    between(n)

            def mixed(bank, tt):
                seen.full += 1
                act.wait_ge(mixed_full, seen.full)
                act.activation(hhi[:, 0:4, tt * P:(tt + 1) * P], tiles_of(bank[tt], 4), ACT.Copy).then_inc(mixed_hi, 1)

            def spare(lin):
                own = lin.banks(At(lin.n - 1))
                return [stream[(2 - own) + tt] for tt in range(TT)]

            columns_of = lambda dst, first: lambda i: dst[:, first + 2 * i:first + 2 * i + 2, :]\
                .rearrange("p a b -> p (a b)")
            rows_of = lambda dst, c: lambda tt: dst[:, tt, c * CH:(c + 1) * CH]

            def mixer_a(st):
                into, outof = st.lins
                places = [rows_of(va, 0), columns_of(qa, 0), columns_of(ka, 0), rows_of(vgate, 0), columns_of(ua, 0)]
                layer(into, lambda c: places[c], lambda c: ACT.Gelu_apprx_tanh if c > 2 else ACT.Copy,
                      after=lambda c: root(slice(None), slice(None), slice(0, 1)) if c == 3 else None)
                seen.aux += 2 + 4
                seen.full += 2
                o_banks = spare(into)

                def between(n):
                    if n == 1:
                        for tt in range(TT):
                            seen.gated += 1
                            act.wait_ge(gated_ready, seen.gated)
                            act.activation(hhi[:, 4:8, tt * P:(tt + 1) * P], tiles_of(gated[tt], 4), ACT.Copy)\
                                .then_inc(mixed_hi, 1)
                    if n == 4:
                        mixed(o_banks, 0)

                attention(BATCHES_A, between)
                seen.aux += 2 * sum(b.banks for b in BATCHES_A)
                mixed(o_banks, 1)
                last_layer(outof, SPLIT)

            def mixer_c(st):
                into, outof = st.lins

                def place(c):
                    if c in (1, 2):
                        return lambda i: conv_in[:, 4 * (c - 1) + 2 * i:4 * (c - 1) + 2 * i + 2, 3:3 + S]
                    if c in (0, 3):
                        return lambda tt: vc[:, tt, 2 * (c // 3):2 * (c // 3) + 2, 0:DV_C]
                    return columns_of(out_gate, 4 * (c - 4))

                def after(c):
                    if c == 2:
                        act.wait_ge(rows_ready, 1)
                        step(act.activation(sum_row[:], sum_row[:], ACT.Exp, scale=-1.0))
                        act.activation(sum_row[:], sum_row[:], ACT.Ln, bias=1.0).then_inc(rows_exp, 1)
                    if c == 3:
                        act.wait_ge(rows_ready, 3)
                        act.activation(forget_row[:], forget_row[:], ACT.Exp, scale=-1.0).then_inc(rows_exp, 1)
                    if c == 4:
                        act.wait_ge(conv_done, 8)
                        act.activation(conv[:], conv[:], ACT.Silu).then_inc(conv_silu, 1)

                layer(into, place, lambda c: ACT.Sigmoid if c > 3 else ACT.Copy, after=after)
                for h in range(HEADS_C):
                    w = mix_w[h % 2]
                    seen.decay += 1
                    act.wait_ge(decay_arg, seen.decay)
                    act.activation(w[:, 0:S], w[:, 0:S], ACT.Exp, bias=gate_cols[:, h:h + 1])
                    act.activation(w[:, S:S + P], w[:, S:S + P], ACT.Exp, bias=gate_cols[:, 8 + h:9 + h])\
                        .then_inc(decay_exp, 1)
                root(slice(None))
                seen.aux += 3 + 4 * HEADS_C + 4
                for pair in range(4):
                    seen.gated += 1
                    act.wait_ge(gated_ready, seen.gated)
                    act.activation(hhi[:, 2 * pair:2 * pair + 2, :],
                                   gated_c[pair % 2][:, :].rearrange("p (a b) -> p a b", a=2), ACT.Copy)\
                        .then_inc(mixed_hi, 1)
                last_layer(outof, SPLIT)

            def mixer_g(st):
                into, br_a, br_b, outof = st.lins

                def place(c):
                    if c < 4:
                        return (rows_of(hv, 0), None, columns_of(hq, 0), rows_of(hgate, 0))[c]
                    if c < 10:
                        return columns_of(aq if c < 7 else ak, 4 * ((c - 4) % 3))
                    if c < 13:
                        return rows_of(av[:, c - 10], 0)
                    return rows_of(gate_a, c - 13) if c < 15 else rows_of(gate_b, c - 15)

                def func(c):
                    return {2: ACT.Silu, 3: ACT.Sigmoid}.get(c, ACT.Sigmoid if c > 12 else ACT.Copy)

                def decay(l):
                    seen.decay += 1
                    act.wait_ge(decay_arg, seen.decay)
                    act.activation(decayed[l % 2][:], decayed[l % 2][:], ACT.Exp).then_inc(decay_exp, 1)

                def after(c):
                    if c == 0 and st.layer:
                        act.wait_ge(bound_arg, 1)
                        act.activation(bound[:], bound[:], ACT.Exp).then_inc(bound_exp, 1)
                    if c == 1:
                        at = At(1)
                        act.wait_ge(block_used, into.done(at))
                        for i in range(2):
                            bank = stream[into.banks(at) + i]
                            act.activation(columns_of(decayed[0], 0)(i), bank[:], ACT.Sigmoid)
                            act.activation(columns_of(hk, 0)(i), bank[:], ACT.Sigmoid, scale=-1.0).then_inc(evicted, 1)
                    if c == 2:
                        seen.f += 1
                        act.wait_ge(f_ready, seen.f)
                        act.activation(decayed[0][:], decayed[0][:], ACT.Ln).then_inc(logf_ready, 1)
                    if 3 <= c <= 10:
                        decay(c - 2)
                    if 4 <= c <= 12:
                        seen.aux += 1 if c == 12 else 2
                    if c == 13:
                        seen.aux += 2
                        root(slice(None))
                    if c == 14:
                        for tt in range(TT):
                            act.wait_ge(aux_full, seen.aux + 1)
                            for h in range(HEADS_G):
                                col = HG_NORM_AT + 4 * st.layer + h
                                a = act.activation(hhi[:, h, tt * P:(tt + 1) * P],
                                                   aux[seen.aux % AUX][:, h * P:(h + 1) * P], ACT.Copy,
                                                   scale=params[:, col:col + 1])
                            a.then_inc(aux_hi, 1)
                            seen.aux += 1

                def beside(lin, first):
                    def within(c, j):
                        n = step_at(lin, c, j, first)
                        if n is None:
                            return
                        if j % 2 == 0:
                            if n < len(BATCHES_G):
                                seen.aux += BATCHES_G[n].banks
                                part = att[n % 2][:, 0:BATCHES_G[n].width]
                                low, total = (small[:, i + 4 * (n % 2):i + 4 * (n % 2) + 1] for i in (0, 8))
                                seen.logits += 1
                                act.wait_ge(logits_ready, seen.logits)
                                act.activation(part, part, ACT.Exp, bias=low, accum_out=total).then_inc(exps_ready, 1)
                                seen.totals += 1
                                act.wait_ge(totals_ready, seen.totals)
                                act.activation(part, part, ACT.Copy, scale=total).then_inc(scaled, 1)
                            if 0 < n <= len(BATCHES_G):
                                seen.aux += BATCHES_G[n - 1].banks
                        elif n >= 2:
                            batch = BATCHES_G[n - 2]
                            h, = batch.heads
                            turn_hi(hhi[:, 4 + h:5 + h, batch.tt * P:(batch.tt + 1) * P], 1)

                    return within

                layer(into, place, func, after=after, within=beside(into, -26))
                layer(br_a, lambda c: rows_of(branch_a, c), within=beside(br_a, 8))

                def turned_hi(half):
                    for tt in range(TT):
                        turn_hi(xhi[:, half * 4:half * 4 + 4, tt * P:(tt + 1) * P], 4)

                layer(br_b, lambda c: None, within=lambda c, j: turned_hi(0) if (c, j) == (1, 1) else None)
                seen.gated += 4
                turned_hi(1)
                last_layer(outof, SPLIT)

            def ffn2(st):
                up, down = st.lins
                h0 = seen.h

                def relu(at):
                    if at.like:
                        act.wait_ge(aux_full, a0 + 2 * (at.like - 1) + 4 * at.turn)
                    evict(up, at, lambda tt: relu_part[at.like % 2][:, tt, :], ACT.Relu)

                split(up, At(0), SPLIT)
                split(up, At(1))
                a0 = seen.aux
                relu(At(0))

                def body(at):
                    split(up, At(at.like + 1, at.turn))
                    relu(at)
                    seen.aux = a0 + 2 * (at.like - 1)
                    for tt in range(TT):
                        turn_hi(hhi[:, bass.ds(4 * (at.c - 1), 4), tt * P:(tt + 1) * P], 4, 4 * at.turn)

                chunks(act, 1, up.n - 1, body)
                seen.aux = a0 + 2 * (up.n - 2)
                ahead(down)
                relu(At(up.n - 1))
                h_turn_hi(4 * (up.n - 2), 4)
                split(down, At(0), SPLIT, SPLIT + 2)
                h_turn_hi(4 * (up.n - 1), 4)
                last_layer(down, SPLIT + 2)
                seen.h = h0 + up.n

            def start_hi(tt, half):
                turn_hi(xhi[:, half * 4:half * 4 + 4, tt * P:(tt + 1) * P], 4)

            start_hi(0, 0)
            split(lins[0], At(0), 0, 1)
            start_hi(0, 1)
            split(lins[0], At(0), 1)
            start_hi(1, 0)
            start_hi(1, 1)
            for st in stages:
                {"ffn1": ffn1, "ab": mixer_a, "c": mixer_c, "hg": mixer_g, "ffn2": ffn2}[st.kind](st)
                norm_act(st)

        @block.vector
        def _(dve):
            step = Steps(dve, dve_step)
            seen = Seen()

            def rest(lin, at, j0=0, j1=None):
                for j in range(j0, lin.kb if j1 is None else j1):
                    b, turn = lin.block(at, j)
                    dve.wait_ge(hi_ready, split_count(b, turn))
                    hi, lo = split_slots(lin, at, j)
                    dve.tensor_tensor(lo, raw[:, b % RAW], hi.bitcast(F32), ALU.subtract).then_inc(lo_ready, 1)

            def ahead(lin):
                if lin is not None:
                    rest(lin, At(0), 0, min(lin.kb, SPLIT))

            def layer(lin, use, within=lambda c, j: None):
                for c in range(lin.n):
                    to, at = (lin, At(c + 1)) if c + 1 < lin.n else (following(lin), At(0))
                    for j in range(lin.kb):
                        within(c, j)
                        if j < to.kb:
                            rest(to, at, j, j + 1)
                    use(c)
                    rest(to, at, lin.kb)

            def turn_lo(hi, lo, n, more=0):
                seen.hi += 1
                dve.wait_ge(aux_hi, seen.hi + more)
                dve.tensor_tensor(lo, tiles_of(aux[seen.aux % AUX], n), hi.bitcast(F32), ALU.subtract)\
                    .then_inc(aux_free, 1)
                seen.aux += 1

            def inverse_root(*where):
                v, r = spread[where], deviation[where]
                seen.std += 1
                dve.wait_ge(std_ready, seen.std)
                step(dve.reciprocal(r, r))
                step(dve.scalar_tensor_tensor(v, v, -0.5, r, ALU.mult, ALU.mult))
                step(dve.tensor_tensor(v, v, r, ALU.mult))
                step(dve.scalar_tensor_tensor(v, v, 1.5, r, ALU.add, ALU.mult))

            def last_layer(st, j0=0):
                lin, kind = st.lins[-1], st.norms[0].kind
                double = 2.0 if st.kind == "ffn1" else 1.0
                src = y if kind == "ln" else x

                def residual(c, tt):
                    part = src[:, tt, c * CH:(c + 1) * CH]
                    if (c, tt) == (1, 0):
                        seen.tiles += 1
                        dve.wait_ge(tile_done, seen.tiles)
                    else:
                        dve.wait_ge(block_used, lin.done(At(c)))
                    seen.sums += 1
                    dve.scalar_tensor_tensor(part, x[:, tt, c * CH:(c + 1) * CH], ALPHA * double if kind == "ln" else 1.0,
                                             stream[lin.banks(At(c)) + tt][:], ALU.mult, ALU.add).then_inc(x_summed, 1)
                    dve.wait_ge(x_summed, seen.sums)
                    dve.sem_inc(evicted, 1)
                    step(dve.bn_stats(stats[:, 0, tt, c, :], part))

                def variance(norm, tt, eps):
                    mean, var, sp = moments[:, tt, 0, 0:1], moments[:, tt, 0, 1:2], spread[:, tt, 0:1]
                    step(dve.bn_aggr(moments[:, tt, 0, :], stats[:, 0, tt, 0:2, :]))
                    if norm.kind == "rms":
                        step(dve.tensor_scalar(var, mean, mean, var, ALU.mult, ALU.add))
                    dve.tensor_scalar(sp, var, eps, None, ALU.add).then_inc(var_ready, 1)

                def inverse(tt):
                    inverse_root(slice(None), tt, slice(0, 1))

                def apply(norm, tt, half):
                    cols = slice(half * CH, (half + 1) * CH)
                    sp = spread[:, tt, 0:1]
                    if norm.kind == "ln":
                        g, b = norm.gain
                        step(dve.scalar_tensor_tensor(y[:, tt, cols], y[:, tt, cols], moments[:, tt, 0, 0:1],
                                                      g[:, cols], ALU.subtract, ALU.mult))
                        return dve.scalar_tensor_tensor(x[:, tt, cols], y[:, tt, cols], sp, b[:, cols],
                                                        ALU.mult, ALU.add)
                    return dve.scalar_tensor_tensor(normed[:, tt, cols], x[:, tt, cols], sp, norm.gain[0][:, cols],
                                                    ALU.mult, ALU.mult)

                def x_turn_lo(tt, half):
                    if st.norms[-1].turned:
                        part = (slice(None), slice(half * 4, half * 4 + 4), slice(tt * P, (tt + 1) * P))
                        turn_lo(xhi[part], xlo[part], 4)

                after = following(lin)
                left = range(0)
                if after is not None and after.b0 not in place:
                    left = range(SPLIT // 2 if after.early else 0, SPLIT)

                def ahead(j):
                    if j in left:
                        rest(after, At(0), j, j + 1)

                rest(lin, At(0), j0)
                middle = min(lin.kb, SPLIT + 2)
                rest(lin, At(1), 0, middle)
                for tt in range(TT):
                    residual(0, tt)
                last_chunk(lin, rest, middle, early=SPLIT // 2)

                def sums(tt):
                    residual(1, tt)
                    for norm in st.norms[:-1]:
                        variance(norm, tt, norm.eps * double ** 2)
                        inverse(tt)
                        for half in range(2):
                            step(apply(norm, tt, half))
                            step(dve.bn_stats(stats[:, 0, tt, half, :], x[:, tt, half * CH:(half + 1) * CH]))
                    norm = st.norms[-1]
                    variance(norm, tt, norm.eps * (double ** 2 if norm.kind == "ln" else 1.0))

                def normalise(tt):
                    inverse(tt)
                    for half in range(2):
                        apply(st.norms[-1], tt, half).then_inc(x_normed, 1)

                dve.wait_ge(gain_in, st.gain_at)
                sums(0)
                normalise(0)
                ahead(0)
                x_turn_lo(0, 0)
                if len(st.norms) == 1:
                    sums(1)
                ahead(1)
                x_turn_lo(0, 1)
                ahead(2)
                ahead(3)
                if len(st.norms) == 2:
                    sums(1)
                normalise(1)
                x_turn_lo(1, 0)
                x_turn_lo(1, 1)
                seen.norm += 1
                dve.wait_ge(x_normed, 2 * TT * seen.norm)
                dve.sem_inc(gain_used, 1)

            def h_turn_lo(first_tile, tiles):
                for tt in range(TT):
                    part = (slice(None), slice(first_tile, first_tile + tiles), slice(tt * P, (tt + 1) * P))
                    turn_lo(hhi[part], hlo[part], tiles)

            def ffn1(st):
                up, down = st.lins
                rest(up, At(0), SPLIT)
                chunks(dve, 1, 7, lambda at: rest(up, at), peel=1)
                if st is stages[0]:
                    copy_params()
                    dve.wait_ge(const_in, 32)

                def product(c):
                    cols = slice(CH // 2, CH) if c == 5 else slice(0, CH)
                    at = c * CH + cols.start - FF1
                    dve.wait_ge(evicted, 2 * (up.c0 + c) + 2)
                    part = silu_gate[:, :, at:at + cols.stop - cols.start]
                    dve.tensor_tensor(part, part, up_part[c % 2][:, :, cols], ALU.mult).then_inc(h_made, 1)

                product(5)
                for c in range(6, up.n):
                    if c + 1 < up.n:
                        rest(up, At(c + 1))
                    else:
                        ahead(down)
                    product(c)
                    h_turn_lo(*FF1_TILES[c - 1])
                rest(down, At(0), SPLIT, SPLIT + 2)
                h_turn_lo(*FF1_TILES[up.n - 1])
                last_layer(st, SPLIT + 2)

            def copy_params():
                dve.wait_ge(aux_full, seen.aux + 1)
                dve.tensor_copy(params[:], aux[seen.aux % AUX][:, 0:PARAM_ROWS]).then_inc(aux_free, 1)
                seen.aux += 1
                dve.wait_ge(aux_free, seen.aux)

            def fold(part, n):
                return part.rearrange("p (a b) -> p a b", a=n)

            def over(part, shape):
                return part.unsqueeze(1).to_broadcast(shape) if part.ndim == 2 else part.to_broadcast(shape)

            def filled(more=0):
                dve.wait_ge(aux_full, seen.aux + 1 + more)
                seen.aux += 1
                return aux[(seen.aux - 1) % AUX]

            def rotate(dst, cos, sin):
                for m in range(2):
                    bank = filled()
                    part = dst[:, 2 * m:2 * m + 2, :]
                    scratch = fold(rope_scratch[:, m * CH:(m + 1) * CH], 2)
                    shape = [P, 2, S]
                    step(dve.tensor_tensor(scratch, fold(bank[:, :], 2), over(sin, shape), ALU.mult))
                    dve.sem_inc(aux_free, 1)
                    step(dve.tensor_tensor(part, part, over(cos, shape), ALU.mult))
                    r = dve.tensor_tensor(part, part, scratch, ALU.add)
                    if m == 1:
                        r.then_inc(roped, 1)
                seen.roped += 1
                dve.wait_ge(roped, seen.roped)

            def masked_logits(batch, n, scale, mask):
                a = att[n % 2]
                low = small[:, 4 * (n % 2):4 * (n % 2) + batch.segments]
                for i in range(batch.banks):
                    bank, width = filled(), batch.bank_width(i)
                    m = mask(batch, i)
                    step(dve.scalar_tensor_tensor(fold(a[:, i * CH:i * CH + width], m.shape[1]),
                                                  fold(bank[:, 0:width], m.shape[1]), scale, m,
                                                  ALU.mult, ALU.add))
                    dve.sem_inc(aux_free, 1)
                step(dve.tensor_reduce(low, fold(a[:, 0:batch.width], batch.segments), AX, ALU.max))
                dve.tensor_scalar(low, low, -1.0, None, ALU.mult).then_inc(logits_ready, 1)

            def copy_weights(batch, n):
                for i in range(batch.banks):
                    bank, width = filled(), batch.bank_width(i)
                    dve.tensor_copy(att_t[n % 2][:, i * CH:i * CH + width], bank[:, 0:width]).then_inc(aux_free, 1)

            def attention(batches, scale, mask, between):
                for n in range(len(batches) + 2):
                    if n > 1:
                        copy_weights(batches[n - 2], n - 2)
                    if n < len(batches):
                        masked_logits(batches[n], n, scale, mask)
                    if 0 < n <= len(batches):
                        batch, k = batches[n - 1], (n - 1) % 2
                        a, w = att[k], batch.width // batch.segments
                        total = small[:, 8 + 4 * k:8 + 4 * k + batch.segments]
                        seen.exps += 1
                        dve.wait_ge(exps_ready, seen.exps)
                        step(dve.reciprocal(total, total))
                        part = fold(a[:, 0:batch.width], batch.segments)
                        dve.tensor_tensor(part, part, over(total.unsqueeze(2), [P, batch.segments, w]), ALU.mult)\
                            .then_inc(probs_ready, 1)
                    between(n)

            def mixed(source, first, tt):
                seen.mixed_hi += 1
                dve.wait_ge(mixed_hi, seen.mixed_hi)
                part = (slice(None), slice(first, first + 4), slice(tt * P, (tt + 1) * P))
                dve.tensor_tensor(hlo[part], source, hhi[part].bitcast(F32), ALU.subtract).then_inc(mixed_lo, 1)

            def spare(lin):
                own = lin.banks(At(lin.n - 1))
                return [stream[(2 - own) + tt] for tt in range(TT)], [stream[own + tt] for tt in range(TT)]

            def mixer_a(st):
                into, outof = st.lins

                def use(c):
                    if c == 1:
                        for half in range(2):
                            bank = filled()
                            dve.tensor_tensor(sgu_wt[:, 4 * half:4 * half + 4], tiles_of(bank, 4),
                                              over(cst("upper"), [P, 4, P]), ALU.mult).then_inc(aux_free, 1)
                    if c in (2, 3):
                        rotate(qa if c == 2 else ka, cst("cos_a"), cst("sin_a"))
                    if c == 3:
                        dve.wait_ge(side_in, 16 * 4)
                        dve.wait_ge(evicted, 2 * (into.c0 + c) + 2)
                        for tt in range(TT):
                            step(dve.bn_stats(stats[:, 0, tt, 0, :], vgate[:, tt]))
                            step(dve.bn_aggr(moments[:, tt, 0, :], stats[:, 0, tt, 0:1, :]))
                            var = dve.tensor_scalar(spread[:, tt, 0:1], moments[:, tt, 0, 1:2], LN_EPS, None, ALU.add)
                        var.then_inc(var_ready, 1)
                        inverse_root(slice(None), slice(None), slice(0, 1))
                        for tt in range(TT):
                            step(dve.scalar_tensor_tensor(vgate[:, tt], vgate[:, tt], moments[:, tt, 0, 0:1],
                                                          sgu_gain[:, 0], ALU.subtract, ALU.mult))
                            v = dve.scalar_tensor_tensor(vgate[:, tt], vgate[:, tt], spread[:, tt, 0:1],
                                                         sgu_gain[:, 1], ALU.mult, ALU.add)
                        v.then_inc(vgate_normed, 1)

                layer(into, use)

                def mask(batch, i):
                    if batch.tt == 0:
                        return over(cst("causal"), [P, 4, P])
                    a, _ = CONST_COLS["zeros"]
                    return over(const[:, a:a + 2 * P], [P, 2, 2 * P])

                o_banks, m_banks = spare(into)

                def between(n):
                    if n == 0:
                        seen.full += 2
                        dve.wait_ge(mixed_full, seen.full)
                        for tt in range(TT):
                            dve.tensor_tensor(fold(gated[tt][:, :], 4), ua[:, :, tt * P:(tt + 1) * P],
                                              tiles_of(m_banks[tt], 4), ALU.mult).then_inc(gated_ready, 1)
                    if n == 2:
                        for tt in range(TT):
                            mixed(fold(gated[tt][:, :], 4), 4, tt)
                    if n == 5:
                        mixed(tiles_of(o_banks[0], 4), 0, 0)

                attention(BATCHES_A, DH_A ** -0.5, mask, between)
                mixed(tiles_of(o_banks[1], 4), 0, 1)
                seen.full += 2
                last_layer(st, SPLIT)

            def mixer_c(st):
                into, outof = st.lins
                step(dve.memset(conv_in[:, :, 0:3], 0.0))
                step(dve.memset(vc[:, :, :, DV_C:DV_C + 1], 1.0))

                def convolve(c, j):
                    if c not in (2, 3):
                        return
                    t = 4 * (c - 2) + j
                    if j == 0:
                        dve.wait_ge(evicted, 2 * (into.c0 + c - 1) + 2)
                    col = lambda at: params[:, at + t:at + t + 1]
                    step(dve.tensor_scalar(conv[:, t], conv_in[:, t, 0:S], col(CONV_W_AT), col(CONV_B_AT),
                                           ALU.mult, ALU.add))
                    for tap in range(1, 4):
                        v = dve.scalar_tensor_tensor(conv[:, t], conv_in[:, t, tap:tap + S],
                                                     col(CONV_W_AT + 8 * tap), conv[:, t], ALU.mult, ALU.add)
                        if tap < 3:
                            step(v)
                    v.then_inc(conv_done, 1)

                def use(c):
                    if c == 1:
                        dve.tensor_copy(gate_tok[:], filled()[:, 0:16]).then_inc(gates_copied, 1)
                        dve.wait_ge(gates_copied, 1)
                        dve.sem_inc(aux_free, 1)
                        dve.wait_ge(evicted, 2 * (into.c0 + c) + 2)
                        step(dve.memset(unit_row[:], 1.0))
                        step(dve.memset(zero_row[:], 0.0))
                    if c == 2:
                        bank = filled()
                        step(dve.tensor_scalar(in_row[:], bank[0:4, 0:S], gate_bias[:, 0:1], None, ALU.add))
                        step(dve.tensor_scalar(forget_row[:], bank[0:4, S:2 * S], gate_bias[:, 1:2], None, ALU.add))
                        dve.sem_inc(aux_free, 1)
                        dve.scalar_tensor_tensor(sum_row[:], forget_row[:], -1.0, forget_row[:], ALU.mult, ALU.max)\
                            .then_inc(rows_ready, 1)
                        dve.wait_ge(rows_exp, 1)
                        step(dve.tensor_scalar(forget_row[:], forget_row[:], 0.0, None, ALU.min))
                        step(dve.tensor_tensor(sum_row[:], forget_row[:], sum_row[:], ALU.subtract))
                        step(dve.tensor_tensor_scan(forget_row[:], unit_row[:], sum_row[:], 0.0, ALU.mult, ALU.add))
                        dve.tensor_tensor(in_row[:], in_row[:], forget_row[:], ALU.subtract).then_inc(rows_ready, 1)
                        dve.wait_ge(rows_ready, 2)
                        step(dve.tensor_tensor_scan(max_row[:], zero_row[:], in_row[:], 0.0, ALU.add, ALU.max))
                        dve.tensor_tensor(forget_row[:], forget_row[:], max_row[:], ALU.add).then_inc(rows_ready, 1)
                    if c == 4:
                        dve.tensor_copy(gate_cols[:], filled()[:, 0:16]).then_inc(aux_free, 1)
                        dve.wait_ge(aux_free, seen.aux)

                layer(into, use, convolve)
                key_mask = cst("causal_key_major")
                a, _ = CONST_COLS["causal_key_major"]

                def normalise(g):
                    banks = [filled(), filled()]
                    den = [small[:, 16 + tt:17 + tt] for tt in range(TT)]
                    out = [heads_out[:, tt, g * DV_C:(g + 1) * DV_C] for tt in range(TT)]
                    sums = [bank[:, DV_C:DV_C + 1] for bank in banks]
                    step(*(dve.tensor_scalar(den[tt], sums[tt], gate_cols[:, tt * 8 + 4 + g:tt * 8 + 5 + g], None,
                                             ALU.max) for tt in range(TT)))
                    step(*(dve.scalar_tensor_tensor(den[tt], sums[tt], -1.0, den[tt], ALU.mult, ALU.max)
                           for tt in range(TT)))
                    step(*(dve.reciprocal(den[tt], den[tt]) for tt in range(TT)))
                    step(*(dve.tensor_scalar(out[tt], banks[tt][:, 0:DV_C], den[tt], None, ALU.mult)
                           for tt in range(TT)))
                    dve.sem_inc(aux_free, 1)
                    dve.sem_inc(aux_free, 1)
                    step(*(dve.bn_stats(stats[:, 1, tt, g, :], out[tt]) for tt in range(TT)))
                    step(*(dve.bn_aggr(moments[:, tt, g, :], stats[:, 1, tt, g:g + 1, :]) for tt in range(TT)))

                for h in range(HEADS_C + 1):
                    if h < HEADS_C:
                        w = mix_w[h % 2]
                        bank = filled()
                        step(dve.tensor_tensor(w[:, 0:S], const[:, a:a + S], bank[:, 0:S], ALU.subtract))
                        dve.tensor_tensor(w[:, S:S + P], key_mask, bank[:, P:S], ALU.subtract).then_inc(decay_arg, 1)
                        seen.decay += 1
                        dve.wait_ge(decay_arg, seen.decay)
                        dve.sem_inc(aux_free, 1)
                        bank = filled()
                        dve.wait_ge(decay_exp, seen.decay)
                        dve.scalar_tensor_tensor(w[:], bank[:, 0:3 * P], DQK_C ** -0.5, w[:], ALU.mult, ALU.mult)\
                            .then_inc(decay_used, 1)
                        dve.wait_ge(decay_used, seen.decay)
                        dve.sem_inc(aux_free, 1)
                    if h:
                        normalise(h - 1)
                dve.tensor_scalar(spread[:], moments[:, :, :, 1], LN_EPS, None, ALU.add).then_inc(var_ready, 1)
                inverse_root(slice(None))
                for h in range(HEADS_C):
                    for tt in range(TT):
                        part = heads_out[:, tt, h * DV_C:(h + 1) * DV_C]
                        v = dve.tensor_scalar(part, part, moments[:, tt, h, 0:1], spread[:, tt, h:h + 1],
                                              ALU.subtract, ALU.mult)
                    v.then_inc(heads_normed, 1)
                for pair in range(4):
                    bank = filled()
                    for k in range(2):
                        kt = 2 * pair + k
                        v = dve.scalar_tensor_tensor(gated_c[pair % 2][:, k * S:(k + 1) * S],
                                                     bank[:, k * S:(k + 1) * S],
                                                     params[:, HEAD_G_AT + kt:HEAD_G_AT + kt + 1], out_gate[:, kt],
                                                     ALU.mult, ALU.mult)
                    v.then_inc(gated_ready, 1)
                    seen.gated += 1
                    dve.wait_ge(gated_ready, seen.gated)
                    dve.sem_inc(aux_free, 1)
                    seen.mixed_hi += 1
                    dve.wait_ge(mixed_hi, seen.mixed_hi)
                    tiles = slice(2 * pair, 2 * pair + 2)
                    dve.tensor_tensor(hlo[:, tiles], fold(gated_c[pair % 2][:, :], 2), hhi[:, tiles].bitcast(F32),
                                      ALU.subtract).then_inc(mixed_lo, 1)
                last_layer(st, SPLIT)

            def mixer_g(st):
                into, br_a, br_b, outof = st.lins
                flat = lambda t: t[:].rearrange("p h t -> p (h t)")

                lb, rest_of = bound[:, 0, :], bound[:, 1, :]
                high = small[:, 20:24]

                def bounds():
                    if st.layer == 0:
                        step(dve.memset(lb, 0.0))
                        step(dve.memset(rest_of, 1.0))
                    else:
                        one = params[:, BOUND_AT:BOUND_AT + 4]
                        two = params[:, BOUND_AT + 4:BOUND_AT + 8]
                        step(dve.tensor_tensor(high, one, two, ALU.max))
                        step(dve.tensor_tensor(lb, two, high, ALU.subtract))
                        dve.tensor_tensor(rest_of, one, high, ALU.subtract).then_inc(bound_arg, 1)

                def forget():
                    if st.layer:
                        dve.wait_ge(bound_exp, 1)
                        step(dve.tensor_tensor(high, lb, rest_of, ALU.add))
                        step(dve.reciprocal(high, high))
                        step(dve.tensor_tensor(lb, lb, high, ALU.mult))
                        step(dve.tensor_tensor(rest_of, rest_of, high, ALU.mult))
                    dve.wait_ge(evicted, 2 * (into.c0 + 1) + 2)
                    for h in range(HEADS_G):
                        f, k = decayed[0][:, h], hk[:, h]
                        step(dve.tensor_scalar(f, f, rest_of[:, h:h + 1], lb[:, h:h + 1], ALU.mult, ALU.add))
                        step(dve.tensor_scalar(k, k, rest_of[:, h:h + 1], None, ALU.mult))
                    dve.tensor_scalar(flat(decayed[0]), flat(decayed[0]), F_MIN, None, ALU.max).then_inc(f_ready, 1)
                    seen.f += 1
                    dve.wait_ge(f_ready, seen.f)

                def sum_decays():
                    keep = decayed[1]
                    step(dve.memset(flat(keep), 1.0))
                    step(dve.memset(flat(keep).rearrange("p (c t) -> p c t", t=CHUNK)[:, :, 0:1], 0.0))
                    dve.wait_ge(logf_ready, seen.f)
                    step(dve.tensor_tensor_scan(flat(decay_sum), flat(keep), flat(decayed[0]), 0.0, ALU.mult, ALU.add))

                def blocks(t, w):
                    return flat(t).rearrange("p (n w) -> p n w", w=w)

                def decay_to(l):
                    to, b = decayed[l % 2], decay_sum
                    half = 2 ** l // 2
                    sub = dve.tensor_tensor
                    if l < LEVELS:
                        t, s = blocks(to, 2 * half), blocks(b, 2 * half)
                        mid = s[:, :, half - 1:half]
                        shape = [P, HEADS_G * S // (2 * half), half]
                        sub(t[:, :, half:], s[:, :, half:], mid.to_broadcast(shape), ALU.subtract)
                        last = sub(t[:, :, 0:half], mid.to_broadcast(shape), s[:, :, 0:half], ALU.subtract)
                    elif l == LEVELS:
                        t = flat(to).rearrange("p (n k w) -> p n k w", k=2, w=CHUNK)
                        s = flat(b).rearrange("p (n k w) -> p n k w", k=2, w=CHUNK)
                        shape = [P, HEADS_G * 2, CHUNK]
                        dve.tensor_copy(t[:, :, 1], s[:, :, 1])
                        last = sub(t[:, :, 0], s[:, :, 0, CHUNK - 1:].to_broadcast(shape), s[:, :, 0], ALU.subtract)
                    else:
                        t = to[:].rearrange("p h (c w) -> p h c w", w=CHUNK)
                        s = b[:].rearrange("p h (c w) -> p h c w", w=CHUNK)
                        shape = [P, HEADS_G, CHUNK]
                        end = lambda c: s[:, :, c, CHUNK - 1:].to_broadcast(shape)
                        dve.tensor_copy(t[:, :, 2], s[:, :, 2])
                        sub(t[:, :, 3], s[:, :, 3], end(2), ALU.add)
                        sub(t[:, :, 1], end(1), s[:, :, 1], ALU.subtract)
                        step(sub(t[:, :, 0], end(0), s[:, :, 0], ALU.subtract))
                        last = sub(t[:, :, 0], t[:, :, 0], end(1), ALU.add)
                    last.then_inc(decay_arg, 1)

                def decay_pairs(l):
                    seen.decay += 1
                    dve.wait_ge(decay_exp, seen.decay)
                    half = min(2 ** l, S) // 2
                    t, q, k = (blocks(x_, 2 * half) for x_ in (decayed[l % 2], hq, hk))
                    dve.tensor_tensor(t[:, :, half:], t[:, :, half:], q[:, :, half:], ALU.mult)
                    dve.tensor_tensor(t[:, :, 0:half], t[:, :, 0:half], k[:, :, 0:half], ALU.mult)\
                        .then_inc(decay_used, 1)

                def pick_pairs(l):
                    if l > LEVELS:
                        bank = filled()
                        dve.tensor_copy(pair_w[:, 2], bank[:]).then_inc(aux_free, 1)
                        seen.pairs += 1
                        dve.wait_ge(aux_free, seen.aux)
                        dve.sem_inc(pairs_ready, 1)
                        return
                    mask = over((level_mask[:, l - 1, :] if l else ident).bitcast(I32), [P, HEADS_G, P])
                    for tt in range(TT):
                        bank = filled()
                        dve.copy_predicated(fold(pair_w[:, tt], HEADS_G), mask, tiles_of(bank, HEADS_G))\
                            .then_inc(aux_free, 1)
                    dve.wait_ge(aux_free, seen.aux)

                def head_norms():
                    for tt in range(TT):
                        bank = filled()
                        dve.tensor_copy(o_hg[:, tt], bank[:]).then_inc(aux_free, 1)
                        dve.wait_ge(aux_free, seen.aux)
                        step(dve.tensor_tensor(o_square[:, tt], o_hg[:, tt], o_hg[:, tt], ALU.mult))
                        step(dve.tensor_reduce(spread[:, tt], fold(o_square[:, tt], HEADS_G), AX, ALU.add))
                    dve.tensor_scalar(spread[:], spread[:], 1.0 / P, RMS_EPS, ALU.mult, ALU.add).then_inc(var_ready, 1)
                    inverse_root(slice(None))
                    for tt in range(TT):
                        part = fold(o_hg[:, tt], HEADS_G)
                        step(dve.tensor_tensor(part, part, over(spread[:, tt].unsqueeze(2), [P, HEADS_G, P]), ALU.mult))
                        v = dve.tensor_tensor(o_hg[:, tt], o_hg[:, tt], hgate[:, tt], ALU.mult)
                    v.then_inc(heads_normed, 1)
                    seen.heads += 1

                def use(c):
                    if c == 0:
                        bounds()
                    if c == 1:
                        forget()
                    if c == 3:
                        sum_decays()
                        step(dve.memset(pair_w[:], 0.0))
                    if 4 <= c <= 12:
                        pick_pairs(c - 4)
                    if 4 <= c <= 11:
                        decay_pairs(c - 3)
                    if 3 <= c <= 10:
                        decay_to(c - 2)
                    if 5 <= c <= 10:
                        group = (c - 5) % 3
                        part = (aq if c < 8 else ak)[0:32, 4 * group:4 * group + 4]
                        other = rope_swap[c % 2]
                        seen.swaps += 1
                        dve.wait_ge(swap_in[c % 2], 32 * ((seen.swaps + 1) // 2))
                        shape = [32, 4, S]
                        step(dve.tensor_tensor(other[:], other[:], over(cst("sin_b", 32), shape), ALU.mult))
                        step(dve.tensor_tensor(part, part, over(cst("cos_b", 32), shape), ALU.mult))
                        dve.tensor_tensor(part, part, other[:], ALU.add).then_inc(roped, 1)
                        seen.roped += 1
                    if c == 13:
                        head_norms()
                    if c == 14:
                        for tt in range(TT):
                            seen.hi += 1
                            dve.wait_ge(aux_hi, seen.hi)
                            for h in range(HEADS_G):
                                col = HG_NORM_AT + 4 * st.layer + h
                                cols = slice(tt * P, (tt + 1) * P)
                                v = dve.scalar_tensor_tensor(hlo[:, h, cols],
                                                             aux[seen.aux % AUX][:, h * P:(h + 1) * P],
                                                             params[:, col:col + 1], hhi[:, h, cols].bitcast(F32),
                                                             ALU.mult, ALU.subtract)
                            v.then_inc(aux_free, 1)
                            seen.aux += 1

                def mask(batch, i):
                    a = CONST_COLS["before_1"][0]
                    if batch.tt == 0:
                        return const[:, a:a + 6 * P].rearrange("p (g k) -> p g k", g=3)[:, :, P:]
                    return const[:, a + i * CH:a + i * CH + batch.bank_width(i)].unsqueeze(1)

                def beside(lin, first):
                    def within(c, j):
                        n = step_at(lin, c, j, first)
                        if n is None:
                            return
                        if j % 2 == 0:
                            if n < len(BATCHES_G):
                                masked_logits(BATCHES_G[n], n, P ** -0.5, mask)
                            if 0 < n <= len(BATCHES_G):
                                copy_weights(BATCHES_G[n - 1], n - 1)
                            if n < len(BATCHES_G):
                                seen.exps += 1
                                dve.wait_ge(exps_ready, seen.exps)
                                total = small[:, 8 + 4 * (n % 2):9 + 4 * (n % 2)]
                                dve.reciprocal(total, total).then_inc(totals_ready, 1)
                        elif n >= 2:
                            batch = BATCHES_G[n - 2]
                            h, = batch.heads
                            part = (slice(None), slice(4 + h, 5 + h), slice(batch.tt * P, (batch.tt + 1) * P))
                            turn_lo(hhi[part], hlo[part], 1)

                    return within

                layer(into, use, beside(into, -26))

                def gated_a(c):
                    cols = slice(c * CH, (c + 1) * CH)
                    dve.wait_ge(evicted, 2 * (br_a.c0 + c) + 2)
                    for tt in range(TT):
                        step(dve.tensor_tensor(branch_a[:, tt, cols], branch_a[:, tt, cols], gate_a[:, tt, cols],
                                               ALU.mult))

                layer(br_a, gated_a, beside(br_a, 8))

                def branches(c):
                    cols = slice(c * CH, (c + 1) * CH)
                    dve.wait_ge(block_used, br_b.done(At(c)))
                    for tt in range(TT):
                        step(dve.tensor_tensor(branch_b[:, tt, cols], stream[br_b.banks(At(c)) + tt][:],
                                               gate_b[:, tt, cols], ALU.mult))
                        dve.sem_inc(evicted, 1)
                        dve.tensor_tensor(gate_a[:, tt, cols], branch_a[:, tt, cols], branch_b[:, tt, cols],
                                          ALU.add).then_inc(gated_ready, 1)

                def turned_lo(half):
                    for tt in range(TT):
                        part = (slice(None), slice(half * 4, half * 4 + 4), slice(tt * P, (tt + 1) * P))
                        turn_lo(xhi[part], xlo[part], 4)

                layer(br_b, branches, lambda c, j: turned_lo(0) if (c, j) == (1, 1) else None)
                turned_lo(1)
                last_layer(st, SPLIT)

            def ffn2(st):
                up, down = st.lins

                def square(at):
                    dve.wait_ge(evicted, 2 * up.chunk(at) + 2)
                    part = relu_part[at.like % 2][:]
                    dve.tensor_tensor(part, part, part, ALU.mult).then_inc(h_made, 1)

                rest(up, At(0), SPLIT)
                rest(up, At(1))
                a0, hi0 = seen.aux, seen.hi
                square(At(0))

                def body(at):
                    rest(up, At(at.like + 1, at.turn))
                    square(at)
                    seen.aux, seen.hi = a0 + 2 * (at.like - 1), hi0 + 2 * (at.like - 1)
                    for tt in range(TT):
                        part = (slice(None), bass.ds(4 * (at.c - 1), 4), slice(tt * P, (tt + 1) * P))
                        turn_lo(hhi[part], hlo[part], 4, 4 * at.turn)

                chunks(dve, 1, up.n - 1, body)
                seen.aux, seen.hi = a0 + 2 * (up.n - 2), hi0 + 2 * (up.n - 2)
                ahead(down)
                square(At(up.n - 1))
                h_turn_lo(4 * (up.n - 2), 4)
                rest(down, At(0), SPLIT, SPLIT + 2)
                h_turn_lo(4 * (up.n - 1), 4)
                last_layer(st, SPLIT + 2)

            def start_lo(tt, half):
                part = (slice(None), slice(half * 4, half * 4 + 4), slice(tt * P, (tt + 1) * P))
                turn_lo(xhi[part], xlo[part], 4)

            start_lo(0, 0)
            rest(lins[0], At(0), 0, 1)
            start_lo(0, 1)
            rest(lins[0], At(0), 1)
            start_lo(1, 0)
            start_lo(1, 1)
            for st in stages:
                {"ffn1": ffn1, "ab": mixer_a, "c": mixer_c, "hg": mixer_g, "ffn2": ffn2}[st.kind](st)

        @block.tensor
        def _(pe):
            side_c = 16 * (1 + 4 * any(st.kind == "ab" for st in stages))
            seen = Seen()

            def aux_bank(more=0):
                if seen.aux >= AUX:
                    pe.wait_ge(aux_free, seen.aux + more - AUX + 1)
                seen.aux += 1
                return aux[(seen.aux - 1) % AUX]

            def rows(lin, at, xh, xl, k0=0, ready=None, hook=None, tile_major=False, tail=None):
                if isinstance(at.turn, int) and lin.chunk(at) < 2:
                    pass
                else:
                    pe.wait_ge(evicted, 2 * (lin.chunk(at) - 1))
                bank = [stream[lin.banks(at) + tt] for tt in range(TT)]
                last = 2 * lin.kb - 1
                order = [(j, tt) for j in range(lin.kb) for tt in range(TT)]
                if tile_major:
                    order = [(j, tt) for tt in range(TT) for j in range(lin.kb)]
                if tail:
                    order = [(j, tt) for j in range(lin.kb - SPLIT) for tt in range(TT)] + \
                        [(j, tt) for tt in range(TT) for j in range(lin.kb - SPLIT, lin.kb)]
                for j, tt in order:
                    if tail and (j, tt) == (lin.kb - 1, 1):
                        tail()
                    b, turn = lin.block(at, j)
                    if hook and tt == 0:
                        hook(j)
                    if ready:
                        pe.wait_ge(*ready(j, tt))
                    if tt == 0:
                        pe.wait_ge(lo_ready, split_count(b, turn))
                    for k in range(BK):
                        kt = j * BK + k
                        cols = slice(tt * P, (tt + 1) * P)
                        hi, lo = xh[:, k0 + kt, cols], xl[:, k0 + kt, cols]
                        wh, wl = (w[:, k] for w in split_slots(lin, at, j))
                        pe.matmul(bank[tt][:], hi, wh, start=kt == 0, stop=False)
                        pe.matmul(bank[tt][:], hi, wl, start=False, stop=False)
                        mm = pe.matmul(bank[tt][:], lo, wh, start=False, stop=kt == last)
                    if tt == TT - 1:
                        mm.then_inc(block_used, 1)
                    elif tail and j == lin.kb - 1:
                        mm.then_inc(tile_done, 1)

            def turn(src, first, n, more=0):
                bank = aux_bank(more)
                for m in range(n):
                    t = pe.transpose(bank[:, m * P:(m + 1) * P], src[:, bass.ds(first + m * P, P)], ident)
                t.then_inc(aux_full, 1)

            def x_turn(src, tt, half):
                if src is not None:
                    if seen.norm:
                        pe.wait_ge(x_normed, 2 * TT * (seen.norm - 1) + 2 * tt + half + 1)
                    else:
                        pe.wait_ge(x_in[tt], 16)
                    turn(src[:, tt], half * 4 * P, 4)

            def x_ready():
                start, src = seen.x_at, seen.x_src

                def ready(j, tt):
                    if (j, tt) == (0, 1) and src:
                        x_turn(src[0], 1, 0)
                        x_turn(src[0], 1, 1)
                    return aux_free, start + 2 * tt + 1 + (j >= SPLIT // 2)

                return ready

            def last_layer(st, xh, xl, ready=None, hook=None):
                lin, norm = st.lins[-1], st.norms[-1]
                src = None if not norm.turned else x if norm.kind == "ln" else normed
                seen.norm += 1
                rows(lin, At(0), xh, xl, 0, ready, hook, tile_major=lin.kb == SPLIT)

                def tail():
                    seen.x_at = seen.aux
                    if len(st.norms) == 1:
                        x_turn(src, 0, 0)

                rows(lin, At(1), xh, xl, tail=tail)
                if len(st.norms) == 2:
                    x_turn(src, 0, 0)
                x_turn(src, 0, 1)
                seen.x_src = [src]

            def h_turn(c, h0):
                first_tile, tiles = FF1_TILES[c]
                pe.wait_ge(h_made, h0 + c - 4)
                for tt in range(TT):
                    turn(silu_gate[:, tt], first_tile * P, tiles)

            def columns(lin, at, ready=None):
                if lin.chunk(at) >= 2:
                    pe.wait_ge(evicted, 2 * (lin.chunk(at) - 1))
                order = [(j, None) for j in range(lin.kb)]
                if ready:
                    order = [(j, tt) for tt in range(TT) for j in range(lin.kb)]
                for j, tt in order:
                    b, turn = lin.block(at, j)
                    tokens = slice(0, S) if tt is None else slice(tt * P, (tt + 1) * P)
                    if ready:
                        pe.wait_ge(*ready(j, tt))
                    if not tt:
                        pe.wait_ge(lo_ready, split_count(b, turn))
                    for k in range(BK):
                        kt = j * BK + k
                        w_hi, w_lo = (w[:, k] for w in split_slots(lin, at, j))
                        for m in range(CH // P):
                            to = stream[lin.banks(at) + m // 2][:, (m % 2) * S + tokens.start:(m % 2) * S + tokens.stop]
                            wh, wl = w_hi[:, m * P:(m + 1) * P], w_lo[:, m * P:(m + 1) * P]
                            first = kt == 0 and m % 2 == 0 and not tt
                            last = kt == lin.kb * BK - 1 and m % 2 == 1 and tt != 0
                            pe.matmul(to, wh, xhi[:, kt, tokens], start=first, stop=False, skip_group_check=True)
                            pe.matmul(to, wh, xlo[:, kt, tokens], start=False, stop=False, skip_group_check=True)
                            mm = pe.matmul(to, wl, xhi[:, kt, tokens], start=False, stop=last, skip_group_check=True)
                    if tt != 0:
                        mm.then_inc(block_used, 1)

            def layer(lin, xh, xl, k0=0, ready=None, major=lambda c: "rows", after=lambda c: None, within=None):
                for c in range(lin.n):
                    if major(c) == "columns":
                        columns(lin, At(c), ready if c == 0 else None)
                        after(c)
                        continue
                    rows(lin, At(c), xh, xl, k0, ready if c == 0 else None,
                         (lambda j: within(c, j)) if within else None, tile_major=c == 0 and lin.kb == 4)
                    after(c)

            def ffn1(st):
                up, down = st.lins
                rows(up, At(0), xhi, xlo, ready=x_ready(), tile_major=True)
                chunks(pe, 1, 7, lambda at: rows(up, at, xhi, xlo), peel=1)
                if st is stages[0]:
                    turn_params()
                h0, a0 = seen.h, seen.aux
                for c in range(6, up.n):
                    if c > 6:
                        rows(up, At(c), xhi, xlo)
                    h_turn(c - 1, h0)
                last_layer(st, hhi, hlo, ready=lambda j, tt: (aux_free, a0 + 2 + 2 * ((j + 1) // 2)),
                           hook=lambda j: h_turn(up.n - 1, h0) if j == 2 else None)
                seen.h += 6

            def turn_params():
                pe.wait_ge(param_in, 16 * 7)
                pe.wait_ge(const_in, 32)
                pe.transpose(aux_bank()[:, 0:PARAM_ROWS], param_rows[:, :], ident[0:PARAM_ROWS, 0:PARAM_ROWS])\
                    .then_inc(aux_full, 1)

            def attention(batches, query, key, value, out_part, banks, between=lambda n: None):
                turned = {}

                def logits(batch):
                    per_bank = CH // batch.keys
                    runs = [(h, g) for h in batch.heads for g in range(batch.groups)]
                    for i in range(batch.banks):
                        bank = aux_bank()
                        for r, (h, g) in enumerate(runs[i * per_bank:(i + 1) * per_bank]):
                            mm = pe.matmul(bank[:, r * batch.keys:(r + 1) * batch.keys],
                                           query(h, g)[:, batch.tt * P:(batch.tt + 1) * P],
                                           key(h, g)[:, 0:batch.keys], start=True, stop=True)
                        mm.then_inc(aux_full, 1)

                def turn_weights(n):
                    batch = batches[n]
                    seen.probs += 1
                    pe.wait_ge(probs_ready, seen.probs)
                    for i in range(batch.banks):
                        turn(att[n % 2], i * CH, batch.bank_width(i) // P)
                    turned[n] = seen.aux

                def products(n):
                    batch = batches[n]
                    pe.wait_ge(aux_free, turned[n])
                    for h in batch.heads:
                        mine = [i for i, piece in enumerate(batch.pieces) if piece[0] == h]
                        for i in mine:
                            _, g, kt = batch.pieces[i]
                            mm = pe.matmul(out_part(banks[batch.tt], h), value(h, g, kt),
                                           att_t[n % 2][:, i * P:(i + 1) * P], start=i == mine[0], stop=i == mine[-1])
                    if n + 1 == len(batches) or batches[n + 1].tt != batch.tt:
                        mm.then_inc(mixed_full, 1)

                for n in range(len(batches) + 2):
                    if n < len(batches):
                        logits(batches[n])
                    if 0 < n <= len(batches):
                        turn_weights(n - 1)
                    if n > 1:
                        products(n - 2)
                    between(n)

            def spare(lin):
                c = At(lin.n - 1)
                pe.wait_ge(evicted, 2 * lin.chunk(c) + 2)
                own = lin.banks(c)
                return [stream[(2 - own) + tt] for tt in range(TT)], [stream[own + tt] for tt in range(TT)]

            def mixer_a(st):
                into, outof = st.lins

                def swap(src):
                    for m in range(2):
                        pe.matmul(aux_bank()[:], cst("swap_a"), src[:, 2 * m:2 * m + 2, :].rearrange("p a b -> p (a b)"),
                                  start=True, stop=True).then_inc(aux_full, 1)

                def after(c):
                    if c == 1:
                        pe.wait_ge(side_in, 16 * 4)
                        for half in range(2):
                            bank = aux_bank()
                            for g in range(4):
                                t = pe.transpose(bank[:, g * P:(g + 1) * P], sgu_w[:, 4 * half + g], ident)
                            t.then_inc(aux_full, 1)
                        seen.sgu = seen.aux
                    if c in (2, 3):
                        pe.wait_ge(evicted, 2 * (into.c0 + c - 1) + 2)
                        swap(qa if c == 2 else ka)

                layer(into, xhi, xlo, ready=x_ready(), after=after,
                      major=lambda c: "columns" if c in (1, 2, 4) else "rows")
                o_banks, m_banks = spare(into)

                def gate_products(n):
                    if n != 0:
                        return
                    seen.vgate += 1
                    pe.wait_ge(vgate_normed, seen.vgate)
                    pe.wait_ge(aux_free, seen.sgu)
                    for tt in range(TT):
                        for g in range(8):
                            to = m_banks[tt][(g % 2) * 64:(g % 2 + 1) * 64, (g // 2) * P:(g // 2 + 1) * P]
                            pe.matmul(to, vgate[:, tt, g * 64:(g + 1) * 64], sgu_wt[:, g], start=True, stop=False)
                            mm = pe.matmul(to, cst("ones")[0:1, 0:64], sgu_bias[0:1, g * P:(g + 1) * P],
                                           start=False, stop=True)
                        mm.then_inc(mixed_full, 1)

                seen.roped += 2
                pe.wait_ge(roped, seen.roped)
                seen.gated += 2
                half = lambda h: slice((h % 2) * 64, (h % 2 + 1) * 64)
                attention(BATCHES_A, lambda h, g: qa[half(h), h // 2], lambda h, g: ka[half(h), h // 2],
                          lambda h, g, kt: va[:, kt, h * 64:(h + 1) * 64],
                          lambda bank, h: bank[half(h), (h // 2) * P:(h // 2 + 1) * P], o_banks, gate_products)
                m0 = seen.mixed
                seen.mixed += 4
                last_layer(st, hhi, hlo, ready=lambda j, tt: (mixed_lo, m0 + 3 + tt))

            def mixer_c(st):
                into, outof = st.lins

                def after(c):
                    if c == 1:
                        pe.wait_ge(side_in, side_c)
                        bank = aux_bank()
                        for tt in range(TT):
                            for k in range(DT):
                                cols = slice(tt * P, (tt + 1) * P)
                                for part in (xhi, xlo):
                                    mm = pe.matmul(bank[:, tt * 8:tt * 8 + 8], part[:, k, cols].bitcast(F32),
                                                   gate_w[:, k, :], start=k == 0 and part is xhi,
                                                   stop=k == DT - 1 and part is xlo)
                        mm.then_inc(aux_full, 1)
                    if c == 2:
                        pe.wait_ge(gates_copied, 1)
                        bank = aux_bank()
                        for tt in range(TT):
                            for i in range(2):
                                at = i * S + tt * P
                                t = pe.transpose(bank[0:4, at:at + P], gate_tok[:, tt * 8 + 4 * i:tt * 8 + 4 * i + 4],
                                                 ident)
                        t.then_inc(aux_full, 1)
                    if c == 4:
                        pe.wait_ge(rows_ready, 3)
                        pe.wait_ge(rows_exp, 2)
                        bank = aux_bank()
                        for tt in range(TT):
                            for i, row in enumerate((in_row, forget_row)):
                                t = pe.transpose(bank[:, tt * 8 + 4 * i:tt * 8 + 4 * i + 4],
                                                 row[:, tt * P:(tt + 1) * P], ident[0:4, 0:4])
                        t.then_inc(aux_full, 1)

                layer(into, xhi, xlo, ready=x_ready(), after=after,
                      major=lambda c: "rows" if c in (0, 3) else "columns")
                pe.wait_ge(conv_silu, 1)
                for h in range(HEADS_C + 1):
                    if h < HEADS_C:
                        q, k = conv[:, h], conv[:, 4 + h]
                        pe.matmul(aux_bank()[:, 0:S], cst("pick_head", 4)[:, h * P:(h + 1) * P], max_row[:, :],
                                  start=True, stop=True).then_inc(aux_full, 1)
                        bank = aux_bank()
                        pe.matmul(bank[:, 0:S], k[:, 0:P], q[:, 0:S], start=True, stop=True)
                        pe.matmul(bank[:, S:S + P], k[:, P:S], q[:, P:S], start=True, stop=True).then_inc(aux_full, 1)
                    if h:
                        g = h - 1
                        w = mix_w[g % 2]
                        seen.decay += 1
                        pe.wait_ge(decay_used, seen.decay)
                        pe.matmul(aux_bank()[:, 0:DV_C + 1], w[:, 0:P], vc[:, 0, g], start=True, stop=True)\
                            .then_inc(aux_full, 1)
                        bank = aux_bank()
                        pe.matmul(bank[:, 0:DV_C + 1], w[:, P:S], vc[:, 0, g], start=True, stop=False)
                        pe.matmul(bank[:, 0:DV_C + 1], w[:, S:S + P], vc[:, 1, g], start=False, stop=True)\
                            .then_inc(aux_full, 1)
                for pair in range(4):
                    seen.heads += 1
                    pe.wait_ge(heads_normed, seen.heads)
                    bank = aux_bank()
                    for k in range(2):
                        for tt in range(TT):
                            kt = 2 * pair + k
                            t = pe.transpose(bank[:, k * S + tt * P:k * S + (tt + 1) * P],
                                             heads_out[:, tt, kt * P:(kt + 1) * P], ident)
                    t.then_inc(aux_full, 1)
                m0 = seen.mixed
                seen.mixed += 4
                seen.gated += 4
                last_layer(st, hhi, hlo, ready=lambda j, tt: (mixed_lo, m0 + j + 1))

            def mixer_g(st):
                into, br_a, br_b, outof = st.lins
                u0, p0, r0 = seen.decay, seen.pairs, seen.roped

                def level(l):
                    if l == 0:
                        pe.wait_ge(f_ready, p0 + 1)
                        left, right = hk, hq
                    else:
                        pe.wait_ge(decay_used, u0 + l)
                        left = right = decayed[l % 2]
                    for tt in range(TT):
                        if l == LEVELS + 1 and tt:
                            break
                        bank = aux_bank()
                        to = slice(P, S) if l == LEVELS + 1 else slice(tt * P, (tt + 1) * P)
                        for h in range(HEADS_G):
                            mm = pe.matmul(bank[:, h * P:(h + 1) * P], left[:, h, tt * P:(tt + 1) * P],
                                           right[:, h, to], start=True, stop=True)
                        mm.then_inc(aux_full, 1)

                def after(c):
                    if 4 <= c <= 12:
                        level(c - 4)
                    if c == 13:
                        pe.wait_ge(pairs_ready, p0 + 1)
                        bank = aux_bank()
                        for h in range(HEADS_G):
                            cols = slice(h * P, (h + 1) * P)
                            mm = pe.matmul(bank[:, cols], pair_w[:, 0, cols], hv[:, 0, cols], start=True, stop=True)
                        mm.then_inc(aux_full, 1)
                        bank = aux_bank()
                        for h in range(HEADS_G):
                            cols = slice(h * P, (h + 1) * P)
                            pe.matmul(bank[:, cols], pair_w[:, 2, cols], hv[:, 0, cols], start=True, stop=False)
                            mm = pe.matmul(bank[:, cols], pair_w[:, 1, cols], hv[:, 1, cols], start=False, stop=True)
                        mm.then_inc(aux_full, 1)
                    if c == 14:
                        seen.heads += 1
                        pe.wait_ge(heads_normed, seen.heads)
                        for tt in range(TT):
                            turn(o_hg[:, tt], 0, 4)
                        seen.o_at = seen.aux

                weights_turned = {}

                def beside(lin, first):
                    def within(c, j):
                        n = step_at(lin, c, j, first)
                        if n is None:
                            return
                        if j % 2 == 0:
                            if n == 0:
                                pe.wait_ge(roped, r0 + 6)
                            if n < len(BATCHES_G):
                                batch = BATCHES_G[n]
                                h, = batch.heads
                                per_bank = CH // batch.keys
                                for i in range(batch.banks):
                                    bank = aux_bank()
                                    for r, g in enumerate(range(GROUPS)[i * per_bank:(i + 1) * per_bank]):
                                        mm = pe.matmul(bank[:, r * batch.keys:(r + 1) * batch.keys],
                                                       aq[:, g * 4 + h, batch.tt * P:(batch.tt + 1) * P],
                                                       ak[:, g * 4 + h, 0:batch.keys], start=True, stop=True)
                                    mm.then_inc(aux_full, 1)
                            if 0 < n <= len(BATCHES_G):
                                seen.scaled += 1
                                pe.wait_ge(scaled, seen.scaled)
                                for i in range(BATCHES_G[n - 1].banks):
                                    turn(att[(n - 1) % 2], i * CH, BATCHES_G[n - 1].bank_width(i) // P)
                                weights_turned[n - 1] = seen.aux
                        elif n >= 2:
                            batch = BATCHES_G[n - 2]
                            h, = batch.heads
                            pe.wait_ge(aux_free, weights_turned[n - 2])
                            bank = aux_bank()
                            for i, (_, g, kt) in enumerate(batch.pieces):
                                mm = pe.matmul(bank[:, 0:P], av[:, g, kt, h * P:(h + 1) * P],
                                               att_t[n % 2][:, i * P:(i + 1) * P],
                                               start=i == 0, stop=i + 1 == len(batch.pieces))
                            mm.then_inc(aux_full, 1)

                    return within

                layer(into, xhi, xlo, ready=x_ready(), after=after,
                      major=lambda c: "columns" if c in (1, 2) or 4 <= c < 10 else "rows", within=beside(into, -26))
                o_at = seen.o_at
                layer(br_a, hhi, hlo, ready=lambda j, tt: (aux_free, o_at), within=beside(br_a, 8))
                o_at = seen.aux

                def turned(half):
                    for tt in range(TT):
                        seen.gated += 1
                        pe.wait_ge(gated_ready, seen.gated)
                        turn(gate_a[:, tt], half * 4 * P, 4)

                layer(br_b, hhi, hlo, k0=4, ready=lambda j, tt: (aux_free, o_at),
                      within=lambda c, j: turned(0) if (c, j) == (1, 1) else None)
                x_at = seen.aux - 2
                turned(1)
                last_layer(st, xhi, xlo, ready=lambda j, tt: (aux_free, x_at + 1 + tt + 2 * (j >= SPLIT // 2)))
                seen.decay, seen.pairs, seen.roped = u0 + LEVELS + 1, p0 + 1, r0 + 6

            def ffn2(st):
                up, down = st.lins
                h0 = seen.h

                def turned(c, more=0, static=None):
                    pe.wait_ge(h_made, h0 + c + 1)
                    for tt in range(TT):
                        turn(relu_part[(c if static is None else static) % 2][:, tt], 0, 4, more)

                rows(up, At(0), xhi, xlo, ready=x_ready(), tile_major=True)
                a0 = seen.aux

                def body(at):
                    rows(up, at, xhi, xlo)
                    seen.aux = a0 + 2 * (at.like - 1)
                    turned(at.c - 1, 4 * at.turn, at.like - 1)

                chunks(pe, 1, up.n - 1, body)
                seen.aux = a0 + 2 * (up.n - 2)
                rows(up, At(up.n - 1), xhi, xlo)
                turned(up.n - 2)
                last_layer(st, hhi, hlo, ready=lambda j, tt: (aux_free, a0 + 2 * (j // 2 + 1)),
                           hook=lambda j: turned(up.n - 1) if j == 2 else None)
                seen.h = h0 + up.n

            pe.wait_ge(ident_in, 16)
            seen.x_at, seen.x_src = 0, [x]
            for half in range(2):
                x_turn(x, 0, half)
            for st in stages:
                {"ffn1": ffn1, "ab": mixer_a, "c": mixer_c, "hg": mixer_g, "ffn2": ffn2}[st.kind](st)



_INS = ['x', 'ln_g', 'ln_b', 'ffn_w_gu', 'ffn_w_down', 'ab_w_in', 'sgu_ln_g', 'sgu_ln_b', 'sgu_w', 'sgu_b', 'ab_w_out', 'c_w_in', 'c_conv_w', 'c_conv_b', 'c_b_i', 'c_b_f', 'c_head_g', 'c_w_out', 'norm1_g_2', 'w_in_2', 'hg_lower_bounds_2', 'hg_norm_g_2', 'w_branch_a_2', 'w_branch_b_2', 'w_out_2', 'norm2_g_2', 'w_up_2', 'w_down_2', 'final_norm_g_2']


def kernel(**inputs):
    import concourse.bacc as bacc
    from concourse.bass_utils import run_bass_kernel_spmd

    nc = bacc.Bacc("TRN2", target_bir_lowering=False, num_devices=1)
    table, masks = constant_tables()
    given = {name: np.ascontiguousarray(inputs[name]) for name in _INS}
    given |= {"const": table, "level_mask": masks}
    io = {name: nc.dram_tensor(name, a.shape, mybir.dt.from_np(a.dtype), kind="ExternalInput").ap()
          for name, a in given.items()}
    out = nc.dram_tensor("out", (1, S, D), F32, kind="ExternalOutput").ap()
    program(nc, io, out, all_stages(io))
    r = run_bass_kernel_spmd(nc, [given], core_ids=[0])
    return r.results[0]["out"]
```
